# Optimizing a Trainium2 kernel written in Bass

```python
import jax, jax.numpy as jnp
from jax import lax
import numpy as np

D_MODEL = 1024
BATCH = 1
SEQ = 1024
DEPTH = 1
DEC_BATCH = 8
DEC_SEQ = 4
PAST_LEN = 8192
PAGE_SIZE = 128

GROUP_DIM = 64
W_A = 6 * GROUP_DIM
W_B = 4 * GROUP_DIM
W_C = 6 * GROUP_DIM
D_MIX = W_A + W_B + W_C
D_IN = 2 * W_A + W_B + 3 * W_C
CONV_A_WIDTH = 31
CONV_A_HIST = CONV_A_WIDTH - 1
POOL_WINDOWS = (2, 4, 8, 16)
POOL_GROUP = W_B // len(POOL_WINDOWS)
POOL_HIST = max(POOL_WINDOWS) - 1
CONV_C_WIDTH = 3
CONV_C_HIST = CONV_C_WIDTH - 1
N_EXPERT_GROUPS = 4
EXPERTS_PER_GROUP = 4
N_EXPERTS = N_EXPERT_GROUPS * EXPERTS_PER_GROUP
TOP_K = 2
D_EXPERT = 512
LN_EPS = 1e-5
DEEPNORM_ALPHA = (2 * DEPTH) ** 0.25
DEEPNORM_BETA = (8 * DEPTH) ** -0.25

kernel_name = 'hybrid_conv_pool_shortconv_hiermoe_step'

def layer_norm(x, g, b):
    xf = x.astype(jnp.float32)
    mu = jnp.mean(xf, axis=-1, keepdims=True)
    var = jnp.mean(jnp.square(xf - mu), axis=-1, keepdims=True)
    return ((xf - mu) * lax.rsqrt(var + LN_EPS) * g.astype(jnp.float32) + b.astype(jnp.float32)).astype(x.dtype)

def causal_dwconv(u_ext, w):
    C = u_ext.shape[-1]
    return lax.conv_general_dilated(u_ext, w[:, None, :].astype(u_ext.dtype), window_strides=(1,), padding='VALID', dimension_numbers=('NWC', 'WIO', 'NWC'), feature_group_count=C)

def multiscale_pool(u_ext, pos0, w_pool):
    Bsz, L, C = u_ext.shape
    T = L - POOL_HIST
    uf = u_ext.astype(jnp.float32)
    cs = jnp.concatenate([jnp.zeros((Bsz, 1, C), jnp.float32), jnp.cumsum(uf, axis=1)], axis=1)
    pos = pos0 + jnp.arange(T)
    cur = uf[:, POOL_HIST:]
    outs = []
    for g, w in enumerate(POOL_WINDOWS):
        lo, hi = g * POOL_GROUP, (g + 1) * POOL_GROUP
        wsum = cs[:, POOL_HIST + 1:, lo:hi] - cs[:, POOL_HIST + 1 - w:POOL_HIST + 1 - w + T, lo:hi]
        cnt = jnp.minimum(pos + 1, w).astype(jnp.float32)[None, :, None]
        d = wsum / cnt - cur[:, :, lo:hi]
        outs.append(jnp.einsum('btc,ce->bte', d, w_pool[g].astype(jnp.float32)))
    return jnp.concatenate(outs, axis=-1).astype(u_ext.dtype)

def mixer(x, st_a, st_b, st_c, pos0, w_in, b_in, conv_a_w, conv_a_b, ln_a_g, ln_a_b, w_pool, pool_scale, conv_c_w, w_out, b_out):
    proj = jnp.einsum('btd,de->bte', x, w_in) + b_in
    s = (W_A, 2 * W_A, 2 * W_A + W_B, 2 * W_A + W_B + W_C, 2 * W_A + W_B + 2 * W_C)
    a_val, a_gate, u_b, c_bg, c_cg, c_h = jnp.split(proj, s, axis=-1)
    a_in = a_val * jax.nn.sigmoid(a_gate)
    a_ext = jnp.concatenate([st_a.astype(a_in.dtype), a_in], axis=1)
    a = causal_dwconv(a_ext, conv_a_w) + conv_a_b
    a = jax.nn.silu(layer_norm(a, ln_a_g, ln_a_b))
    b_ext = jnp.concatenate([st_b.astype(u_b.dtype), u_b], axis=1)
    bo = multiscale_pool(b_ext, pos0, w_pool) * pool_scale
    c_in = c_cg * c_h
    c_ext = jnp.concatenate([st_c.astype(c_in.dtype), c_in], axis=1)
    co = c_bg * causal_dwconv(c_ext, conv_c_w)
    y = jnp.einsum('bte,ed->btd', jnp.concatenate([a, bo, co], axis=-1), w_out) + b_out
    return (y, a_ext[:, -CONV_A_HIST:], b_ext[:, -POOL_HIST:], c_ext[:, -CONV_C_HIST:])

def hier_moe(x, w_rg, b_rg, w_re, b_re, w_gate, w_up, w_down):
    Bsz, T, D = x.shape
    xt = x.reshape(Bsz * T, D)
    N = xt.shape[0]
    g_logits = (xt @ w_rg + b_rg).astype(jnp.float32)
    g_prob = jax.nn.softmax(g_logits, axis=-1)
    g_idx = jnp.argmax(g_logits, axis=-1)
    g_p = jnp.take_along_axis(g_prob, g_idx[:, None], axis=-1)
    e_logits = (xt @ w_re + b_re).astype(jnp.float32).reshape(N, N_EXPERT_GROUPS, EXPERTS_PER_GROUP)
    e_sel = jnp.take_along_axis(e_logits, g_idx[:, None, None], axis=1)[:, 0]
    top_v, top_i = lax.top_k(e_sel, TOP_K)
    top_w = jax.nn.softmax(top_v, axis=-1) * g_p
    expert_id = g_idx[:, None] * EXPERTS_PER_GROUP + top_i
    gate = jnp.sum(jax.nn.one_hot(expert_id, N_EXPERTS, dtype=jnp.float32) * top_w[..., None], axis=1).astype(x.dtype)
    y = jnp.zeros_like(xt)
    for e in range(N_EXPERTS):
        h = jax.nn.silu(xt @ w_gate[e]) * (xt @ w_up[e])
        y = y + gate[:, e:e + 1] * (h @ w_down[e])
    return y.reshape(Bsz, T, D)

def trunk(x, st_a, st_b, st_c, pos0, w_in, b_in, conv_a_w, conv_a_b, ln_a_g, ln_a_b, w_pool, pool_scale, conv_c_w, w_out, b_out, ln1_g, ln1_b, w_rg, b_rg, w_re, b_re, w_gate, w_up, w_down, ln2_g, ln2_b):
    na, nb, nc = [], [], []
    for l in range(DEPTH):
        m, sa, sb, sc = mixer(x, st_a[l], st_b[l], st_c[l], pos0, w_in[l], b_in[l], conv_a_w[l], conv_a_b[l], ln_a_g[l], ln_a_b[l], w_pool[l], pool_scale[l], conv_c_w[l], w_out[l], b_out[l])
        x = layer_norm(DEEPNORM_ALPHA * x + m, ln1_g[l], ln1_b[l])
        x = layer_norm(DEEPNORM_ALPHA * x + hier_moe(x, w_rg[l], b_rg[l], w_re[l], b_re[l], w_gate[l], w_up[l], w_down[l]), ln2_g[l], ln2_b[l])
        na.append(sa)
        nb.append(sb)
        nc.append(sc)
    return (x, jnp.stack(na), jnp.stack(nb), jnp.stack(nc))

def setup_inputs(seed: int = 0) -> dict:
    key = jax.random.key(seed)
    ks = jax.random.split(key, 32)
    f = jnp.float32
    nrm = lambda k, shape, s: jax.random.normal(k, shape, f) * s
    L = DEPTH
    return {
        'x_prompt': nrm(ks[0], (BATCH, SEQ, D_MODEL), 1.0),
        'x_sample': nrm(ks[1], (DEC_BATCH, DEC_SEQ, D_MODEL), 1.0),
        'state_conv_a': nrm(ks[2], (L, DEC_BATCH, CONV_A_HIST, W_A), 0.5),
        'state_pool_b': nrm(ks[3], (L, DEC_BATCH, POOL_HIST, W_B), 1.0),
        'state_conv_c': nrm(ks[4], (L, DEC_BATCH, CONV_C_HIST, W_C), 0.5),
        'w_in': nrm(ks[5], (L, D_MODEL, D_IN), D_MODEL ** -0.5),
        'b_in': nrm(ks[6], (L, D_IN), 0.02),
        'conv_a_w': nrm(ks[7], (L, CONV_A_WIDTH, W_A), CONV_A_WIDTH ** -0.5),
        'conv_a_b': nrm(ks[8], (L, W_A), 0.02),
        'ln_a_g': 1.0 + nrm(ks[9], (L, W_A), 0.02),
        'ln_a_b': nrm(ks[10], (L, W_A), 0.02),
        'w_pool': nrm(ks[11], (L, len(POOL_WINDOWS), POOL_GROUP, POOL_GROUP), POOL_GROUP ** -0.5),
        'pool_scale': 1.0 + nrm(ks[12], (L, W_B), 0.1),
        'conv_c_w': nrm(ks[13], (L, CONV_C_WIDTH, W_C), CONV_C_WIDTH ** -0.5),
        'w_out': nrm(ks[14], (L, D_MIX, D_MODEL), DEEPNORM_BETA * D_MIX ** -0.5),
        'b_out': nrm(ks[15], (L, D_MODEL), 0.02),
        'ln1_g': 1.0 + nrm(ks[16], (L, D_MODEL), 0.02),
        'ln1_b': nrm(ks[17], (L, D_MODEL), 0.02),
        'w_router_group': nrm(ks[18], (L, D_MODEL, N_EXPERT_GROUPS), D_MODEL ** -0.5),
        'b_router_group': nrm(ks[19], (L, N_EXPERT_GROUPS), 0.01),
        'w_router_expert': nrm(ks[20], (L, D_MODEL, N_EXPERTS), D_MODEL ** -0.5),
        'b_router_expert': nrm(ks[21], (L, N_EXPERTS), 0.01),
        'w_gate': nrm(ks[22], (L, N_EXPERTS, D_MODEL, D_EXPERT), D_MODEL ** -0.5),
        'w_up': nrm(ks[23], (L, N_EXPERTS, D_MODEL, D_EXPERT), D_MODEL ** -0.5),
        'w_down': nrm(ks[24], (L, N_EXPERTS, D_EXPERT, D_MODEL), DEEPNORM_BETA * D_EXPERT ** -0.5),
        'ln2_g': 1.0 + nrm(ks[25], (L, D_MODEL), 0.02),
        'ln2_b': nrm(ks[26], (L, D_MODEL), 0.02),
    }

def reference(x_prompt, x_sample, state_conv_a, state_pool_b, state_conv_c, w_in, b_in, conv_a_w, conv_a_b, ln_a_g, ln_a_b, w_pool, pool_scale, conv_c_w, w_out, b_out, ln1_g, ln1_b, w_router_group, b_router_group, w_router_expert, b_router_expert, w_gate, w_up, w_down, ln2_g, ln2_b):
    params = (w_in, b_in, conv_a_w, conv_a_b, ln_a_g, ln_a_b, w_pool, pool_scale, conv_c_w, w_out, b_out, ln1_g, ln1_b, w_router_group, b_router_group, w_router_expert, b_router_expert, w_gate, w_up, w_down, ln2_g, ln2_b)
    dt = x_prompt.dtype
    za = jnp.zeros((DEPTH, BATCH, CONV_A_HIST, W_A), dt)
    zb = jnp.zeros((DEPTH, BATCH, POOL_HIST, W_B), dt)
    zc = jnp.zeros((DEPTH, BATCH, CONV_C_HIST, W_C), dt)
    y_prompt, pa, pb, pc = trunk(x_prompt, za, zb, zc, 0, *params)
    y_sample, sa, sb, sc = trunk(x_sample, state_conv_a, state_pool_b, state_conv_c, PAST_LEN, *params)
    return (y_prompt, y_sample, pa, sa, pb, sb, pc, sc)


_drawn_inputs = setup_inputs


def setup_inputs(seed=0):
    import zlib

    import numpy as np

    out = dict(_drawn_inputs(seed))
    spreads = {}
    factors = {'conv_a_b': 4.577,
     'ln_a_g': 20.035,
     'ln_a_b': 41.254,
     'b_out': 11.719,
     'b_router_group': 22.072,
     'b_router_expert': 20.41,
     'ln2_g': 21.992,
     'ln2_b': 21.958,
     'pool_scale': 3.786,
     'state_conv_c': 2.714}
    for name, (base, spread) in spreads.items():
        noise = np.random.default_rng([zlib.crc32(name.encode()), seed]).standard_normal(out[name].shape)
        drawn = base * np.exp(spread * noise) if base else spread * noise
        out[name] = __import__('jax').numpy.asarray(drawn.astype(out[name].dtype))
    for name, factor in factors.items():
        out[name] = (out[name] * factor).astype(out[name].dtype)
    return out
```

```python
from contextlib import ExitStack

import concourse.bass as bass
from concourse import mybir

F32 = mybir.dt.float32
F32R = mybir.dt.float32r
BF16 = mybir.dt.bfloat16
I32 = mybir.dt.int32
U32 = mybir.dt.uint32
ALU = mybir.AluOpType
ACT = mybir.ActivationFunctionType
AX = mybir.AxisListType.X
ds = bass.ds

P = 128
D = 1024
SEQ, DECB, DECT = 1024, 8, 4
NS = DECB * DECT
TOK = SEQ + NS
KD = D // P
NT = (TOK + P - 1) // P
GRP = TOK // 3
LASTP = SEQ - 2 * GRP
WA, WB, WC = 384, 256, 384
CA, CB, CC = WA // P, WB // P, WC // P
D_IN = 2 * WA + WB + 3 * WC
NCH = D_IN // P
TAPS, HA = 31, 30
HB = 15
HC = 2
NG, EPG = 4, 4
NE = NG * EPG
F = 512
KF = F // P
EPS = 1e-5
ALPHA = 2.0 ** 0.25
MAXT = (2 * TOK + NE * (P - 1)) // P
NTAB = MAXT + 2
YT = MAXT + 1

BLK_VAL, BLK_GATE, BLK_U, BLK_BG, BLK_CG, BLK_H = 0, CA, 2 * CA, 2 * CA + CB, 2 * CA + CB + CC, 2 * CA + CB + 2 * CC
ORDER = ([b for c in range(CA) for b in (BLK_VAL + c, BLK_GATE + c)] + [BLK_U, BLK_U + 1]
         + [b for c in range(CC) for b in (BLK_CG + c, BLK_H + c)] + [BLK_BG + c for c in range(CC)])

LA, LAS = HA + SEQ, HA + DECT
EXTA = CA * (LA + DECB * LAS)
LB, LBS = HB + SEQ, HB + DECT
LC, LCS = HC + SEQ, HC + DECT
OFF_B = 2 * 2 * D
OFF_C = OFF_B + CB * (LB + DECB * LBS)
OFF_STAGE = OFF_C + CC * (LC + DECB * LCS)
OFF_BC = 4 * 2 * D
RAWW = OFF_BC + 3 * D


class Tally:

    def __init__(self, sem):
        self.sem, self.n = sem, 0

    def __call__(self, ins, by=1):
        ins.then_inc(self.sem, by)
        self.n = self.n + by
        return self.n


def build(nc, x_prompt, x_sample, st_a, st_b, st_c, w_in, b_in, conv_a_w, conv_a_b, ln_a_g, ln_a_b,
          w_pool, pool_scale, conv_c_w, w_out, b_out, ln1_g, ln1_b, w_rg, b_rg, w_re, b_re,
          w_gate, w_up, w_down, ln2_g, ln2_b, y_p, y_s, na_p, na_s, nb_p, nb_s, nc_p, nc_s):
    x1_dram = nc.dram_tensor("x1_rows", (TOK, D), F32).ap()
    y_dram = nc.dram_tensor("expert_rows", (YT * P, D), F32).ap()
    xp, xs = x_prompt[0], x_sample.rearrange("b t d -> (b t) d")
    yp, ys = y_p[0], y_s.rearrange("b t d -> (b t) d")

    with ExitStack() as ctx:
        def sb(name, shape, dt):
            return ctx.enter_context(nc.sbuf_tensor(name, shape, dt))

        sems = {}

        def S(name):
            if name not in sems:
                sems[name] = ctx.enter_context(nc.semaphore(name))
            return sems[name]

        BIG = sb("BIG", [P, 2 * KD * TOK], F32R)
        WD = sb("WD", [P, 2 * KF * D], F32R)
        TH = sb("TH", [P, 3 * D], F32R)
        RAW = sb("RAW", [P, RAWW], F32)
        MIX = sb("MIX", [P, KD * TOK], F32)
        F2 = sb("F2", [P, 4 * TOK], F32)
        C = sb("C", [P, 912], F32)
        TRI = sb("TRI", [P, 2, P], BF16)
        NTI = sb("NTI", [P, 2 * NE + 1], I32)
        PS = ctx.enter_context(nc.psum_tensor("PS", [P, 8, 512], F32))

        col = [0]

        def const(n):
            a = col[0]
            col[0] += n
            assert col[0] <= 912
            return C[:, a:a + n]

        ident, ones = const(P), const(P)
        wpool = const(CB * P)
        pcA, pcB = const(TAPS * CA), const(37)
        wrt = const(KD * (NG + NE))
        brt = const(NG + NE)
        winv, wmin, tpos, rcnt = const(CB), const(CB), const(HB + 1), const(CB * (HB + 1))
        epsc, zc = const(1), const(1)

        def pcol(block):
            return pcB[:, block:block + 1] if isinstance(block, int) else pcB[:, ds(block, 1)]

        COL_CB, COL_G, COL_B, COL_PS, COL_CW = NCH, NCH + 3, NCH + 6, NCH + 9, NCH + 11

        xT = BIG[:, :].rearrange("p (s k t) -> p s k t", s=2, k=KD)
        wo = BIG[:, 0:2 * KD * D].rearrange("p (s k n) -> p s k n", s=2, k=KD)
        win = WD[:, 0:4 * D].rearrange("p (q s k m) -> p q s k m", q=2, s=2, k=KD)
        mhl = WD[:, 4 * D:8 * D].rearrange("p (q s k m) -> p q s k m", q=2, s=2, k=KD)
        wd = WD[:, :].rearrange("p (s k n) -> p s k n", s=2, k=KF)
        xe = TH[:, 0:2 * D].rearrange("p (s k m) -> p s k m", s=2, k=KD)
        he = TH[:, 2 * D:3 * D].rearrange("p (s k m) -> p s k m", s=2, k=KF)

        def ext(off, chunks, length, slen):
            a = RAW[:, off:off + chunks * length].rearrange("p (c t) -> p c t", c=chunks)
            o = off + chunks * length
            b = RAW[:, o:o + chunks * DECB * slen].rearrange("p (c b t) -> p c b t", c=chunks, b=DECB)
            return a, b

        aP, aS = ext(0, CA, LA, LAS)
        bP, bS = ext(OFF_B, CB, LB, LBS)
        cP, cS = ext(OFF_C, CC, LC, LCS)
        unit = [RAW[:, u * 2 * D:(u + 1) * 2 * D] if u < 4 else MIX[:, (u - 4) * 2 * D:(u - 3) * 2 * D]
                for u in range(6)]
        bc_g1, bc_b1, bc_bo = (RAW[:, OFF_BC + i * D:OFF_BC + (i + 1) * D] for i in range(3))
        mix = MIX[:, :].rearrange("p (c t) -> p c t", c=KD)
        gs = F2[:, 0:TOK]
        xrow = [F2[:, 0:D], F2[:, TOK:TOK + D]]
        wraw = [F2[:, 2 * TOK:2 * TOK + D], F2[:, 2 * TOK + D:2 * TOK + 2 * D]]
        trow = [F2[:, i * TOK:i * TOK + D] for i in range(3)]
        x1T = F2[:, 3 * TOK:3 * TOK + D].rearrange("p (k m) -> p k m", k=KD)
        moff = [4 * D]

        def mx(n):
            a = moff[0]
            moff[0] += n
            assert moff[0] <= KD * TOK
            return MIX[:, a:a + n]

        def bank(b, n=512, rows=P):
            return PS[0:rows, b, 0:n]

        def rows_of(i):
            return P if i < NT - 1 else TOK - (NT - 1) * P


        L = wpool[:, 0:NT * 20].rearrange("p (i c) -> p i c", i=NT)
        bn = [wpool[:, 180 + 18 * q:192 + 18 * q].rearrange("p (h s) -> p h s", h=2) for q in range(2)]
        mv = [wpool[:, 192 + 18 * q:194 + 18 * q] for q in range(2)]
        sd = [wpool[:, 194 + 18 * q:195 + 18 * q] for q in range(2)]
        rstd = [wpool[:, 195 + 18 * q:196 + 18 * q] for q in range(2)]
        nmr = [wpool[:, 196 + 18 * q:197 + 18 * q] for q in range(2)]

        ig = mx(P)
        it = mx(NTAB)
        tokid = mx(NT)
        dsc = mx(EPG)
        iint = mx(P).bitcast(I32)
        g9 = [mx(NT) for _ in range(10)]
        g36 = [mx(NT * NG).rearrange("p (i c) -> p i c", i=NT) for _ in range(8)]
        g144 = [mx(NT * NE).rearrange("p (i g j) -> p i g j", i=NT, g=NG) for _ in range(4)]
        Mb = mx(NT * NE // 2).bitcast(BF16).rearrange("p (i e) -> p i e", i=NT)
        ntf, inc, exc, ci, ci2 = (mx(NE) for _ in range(5))
        r18 = [mx(2 * NT).rearrange("p (k i) -> p k i", k=2) for _ in range(9)]
        wgt = mx(2 * NT).rearrange("p (k i) -> p k i", k=2)
        slot = mx(2 * NT).bitcast(U32).rearrange("p (k i) -> p k i", k=2)
        ohp = [mx(P) for _ in range(2)]
        oht = [mx(NTAB) for _ in range(2)]
        table = mx(NTAB).bitcast(U32)
        idxc = mx(1).bitcast(U32)
        carrier = mx(3)
        xg, yrow, hid = F2[:, 0:D], F2[:, TOK:TOK + D], F2[:, 2 * TOK:2 * TOK + F]
        x1c = [RAW[:, i * D:(i + 1) * D] for i in range(8)] + [RAW[:, OFF_BC:OFF_BC + D]]
        bc_g2, bc_b2 = RAW[:, OFF_BC + D:OFF_BC + 2 * D], RAW[:, OFF_BC + 2 * D:OFF_BC + 3 * D]
        yg = [MIX[:, i * D:(i + 1) * D] for i in range(4)] + [F2[:, i * TOK:i * TOK + D] for i in range(4)]

        out_a = RAW[:, OFF_STAGE:OFF_STAGE + 3 * WA].rearrange("p (s n) -> p s n", s=3)
        out_ap, out_c = wraw[1][:, 0:WA], wraw[1][:, WA:WA + WC]
        out_b = F2[:, TOK:TOK + 3 * WB].rearrange("p (s n) -> p s n", s=3)
        out_cp = RAW[:, OFF_STAGE + 3 * WA:OFF_STAGE + 4 * WA]
        PER_A, PER_B = P // LAS, P // LBS
        squares = F2[:, TOK:2 * TOK].rearrange("p (c t) -> p c t", c=CA)
        stdev = RAW[:, OFF_STAGE + 3 * WA:OFF_STAGE + 3 * WA + GRP]

        vec_rows = MIX[:, 0:2 * P].rearrange("p (s n) -> p s n", s=2)
        hist_a = MIX[:, 2 * P:2 * P + 2 * WA].rearrange("p (s n) -> p s n", s=2)
        hist_b = MIX[:, 2 * P + 2 * WA:2 * P + 2 * WA + WB]
        hist_c = MIX[:, 2 * P + 2 * WA + WB:2 * P + 3 * WA + WB]

        jobs = ([(f"m{g}", "centred", 3 * (g + 1)) for g in range(3)]
                + [(f"a{j}", "state_out_a", j + 1) for j in range(3)]
                + [(f"p{c}{g}", "pool_out", 3 * c + g + 1) for c in range(CB) for g in range(3)]
                + [(f"v{g}", "stdev_a", g + 1) for g in range(3)]
                + [(n, "state_out_bc", j + 1) for j, n in enumerate(("b0", "b1", "b2", "c0", "c1", "a3"))])
        job_no = {name: j for j, (name, _, _) in enumerate(jobs)}
        MB = {name: 6 + j % 2 for j, (name, _, _) in enumerate(jobs)}

        def misc_ready(eng, name):
            eng.wait_ge(S("misc_done"), job_no[name] + 1)

        N_U, N_C, N_BG = 2 * CA, 2 * CA + CB, 2 * CA + CB + 2 * CC

        LO_DVE, LO_POOL = (0, 2, 3, 4), (1, 5)

        def wait_lo(eng, e, u):
            if u in LO_DVE:
                eng.wait_ge(S("unit_lo_dve"), len(LO_DVE) * e + LO_DVE.index(u) + 1)
            else:
                eng.wait_ge(S("unit_lo_pool"), len(LO_POOL) * e + LO_POOL.index(u) + 1)

        def unit_parts(u):
            if u < 4:
                return wo[:, 0, 2 * u:2 * u + 2, :], wo[:, 1, 2 * u:2 * u + 2, :]
            return wd[:, 0, 2 * (u - 4):2 * (u - 3), :], wd[:, 1, 2 * (u - 4):2 * (u - 3), :]

        def unit_raw(u):
            return unit[u].rearrange("p (k n) -> p k n", k=2)

        def first_last(eng, e):
            return [eng.value_load(NTI[0:1, ds(e + h * NE, 1)], min_val=0, max_val=MAXT - 1) for h in range(2)]

        def expert_tiles(eng, tile):
            eng.wait_ge(S("counts_ready"), 3)

            def one(e, splits):
                first, last = first_last(eng, e)
                with eng.If(first < last):
                    with eng.Fori(first, last) as t:
                        tile(t, e, False)
                tile(last, e, splits)
            with eng.Fori(0, NE - 1) as e:
                one(e, True)
            one(NE - 1, False)

        def load_unit(sp, e, u):
            if u < 4:
                for h, w in enumerate((w_gate, w_up)):
                    src = w[0, ds(e, 1)].rearrange("a (p k) f -> p (a k) f", p=P)[:, 2 * u:2 * u + 2, :]
                    sp.dma_start(unit_raw(u)[:, :, h * F:(h + 1) * F], src).then_inc(S(f"unit_raw{u}"), 16)
            else:
                v = u - 4
                src = w_down[0, ds(e, 1), v * 2 * P:(v + 1) * 2 * P, :].rearrange("a (k p) n -> p (a k) n", p=P)
                sp.dma_start(unit_raw(u), src).then_inc(S(f"unit_raw{u}"), 16)

        block = ctx.enter_context(nc.Block())

        @block.sync
        def _(sp):
            def load_x(i, q):
                M = rows_of(i) if isinstance(i, int) else P
                src = xs if isinstance(i, int) and i == NT - 1 else xp[ds(i * P, P), :]
                sp.dma_start(xrow[q][0:M], src).then_inc(S(f"x_rows{q}"), 16)

            def load_w(n, q, block_):
                src = w_in[0, :, ds(block_ * P, P)].rearrange("(k p) m -> p k m", p=P)
                sp.dma_start(wraw[q].rearrange("p (k m) -> p k m", k=KD), src).then_inc(S(f"win_raw{q}"), 16)

            load_x(0, 0)
            load_x(1, 1)
            load_w(0, 0, ORDER[0])
            load_w(1, 1, ORDER[1])
            with sp.Fori(1, 4) as i:
                for q in range(2):
                    sp.wait_ge(S("x_turned"), 2 * i + q - 1)
                    load_x(2 * i + q, q)
            sp.wait_ge(S("x_turned"), NT - 2)
            load_x(NT - 1, 0)

            def win_pair(n, b0, b1):
                for q, b in enumerate((b0, b1)):
                    sp.wait_ge(S("win_lo"), n + q - 1)
                    load_w(n + q, q, b)
            with sp.Fori(1, CA) as c:
                win_pair(2 * c, BLK_VAL + c, BLK_GATE + c)
            win_pair(N_U, BLK_U, BLK_U + 1)
            with sp.Fori(0, CC) as c:
                win_pair(N_C + 2 * c, BLK_CG + c, BLK_H + c)
            win_pair(N_BG, BLK_BG, BLK_BG + 1)
            sp.wait_ge(S("win_lo"), N_BG + 1)
            load_w(N_BG + 2, 0, BLK_BG + 2)

            sp.wait_ge(S("state_out_a"), 3)
            for b in range(DECB):
                r = (b % PER_A) * LAS + DECT
                sp.dma_start(na_s[0, b], out_a[r:r + HA, b // PER_A, :]).then_inc(S("state_stored_a"), 16)

            def load_wo(u):
                sp.dma_start(unit_raw(u), w_out[0, u * 2 * P:(u + 1) * 2 * P, :].rearrange("(k p) n -> p k n", p=P)
                             ).then_inc(S(f"wo_raw{u}"), 16)

            def load_t(i):
                sp.dma_start(trow[(i + 2) % 3][0:rows_of(i)], xs if i == NT - 1 else xp[i * P:(i + 1) * P, :]
                             ).then_inc(S(f"x_again{i % 3}"), 16)
            sp.wait_ge(S("state_out_bc"), 6)
            for u in range(3):
                load_wo(u)
            for b in range(DECB):
                r = (b % PER_B) * LBS + DECT
                sp.dma_start(nb_s[0, b], out_b[r:r + HB, b // PER_B, :]).then_inc(S("state_stored_bc"), 16)
                r = b * LCS + DECT
                sp.dma_start(nc_s[0, b], out_c[r:r + HC, :]).then_inc(S("state_stored_bc"), 16)
            sp.dma_start(nb_p[0, 0], out_b[0:HB, 2, :]).then_inc(S("state_stored_bc"), 16)
            sp.dma_start(nc_p[0, 0], out_cp[0:HC, :]).then_inc(S("state_stored_bc"), 16)
            sp.dma_start(na_p[0, 0], out_ap[0:HA, :]).then_inc(S("state_stored_bc"), 16)
            sp.wait_ge(S("short_conv"), 27)
            load_wo(3)
            sp.wait_ge(S("win_lo"), NCH)
            load_t(0)
            sp.wait_ge(S("state_stored_a"), 16 * DECB)
            sp.wait_ge(S("state_stored_bc"), 16 * (2 * DECB + 3))
            for dst, src in ((bc_bo, b_out), (bc_g1, ln1_g), (bc_b1, ln1_b)):
                sp.dma_start(dst, src[0:1, :].to_broadcast((P, D))).then_inc(S("ln1_rows"), 16)
            sp.wait_ge(S("short_done"), 6)
            load_t(1)
            load_t(2)
            for i in range(NT):
                sp.wait_ge(S("x1_ready"), i + 1)
                M = rows_of(i)
                sp.dma_start(x1_dram[i * P:i * P + M, :], trow[(i + 2) % 3][0:M]).then_inc(S("x1_stored"), 16)
                if i + 3 < NT:
                    sp.wait_ge(S("x1_stored"), 16 * (i + 1))
                    sp.wait_ge(S("x1_turned"), i + 1)
                    load_t(i + 3)
                if i == 0:
                    for u in range(4):
                        sp.wait_ge(S("wo_lo"), u + 1)
                        load_unit(sp, 0, u)
            sp.wait_ge(S("mix_lo"), NT)
            for u in (4, 5):
                load_unit(sp, 0, u)

            with sp.Fori(1, NE) as e:
                for u in range(6):
                    wait_lo(sp, e - 1, u)
                    load_unit(sp, e, u)
            sp.wait_ge(S("counts_ready"), 3)
            _first, last = first_last(sp, NE - 1)
            with sp.Fori(last + 1, YT) as t:
                sp.dma_start(y_dram[ds(t * P, P), :], x1_dram[0:P, :]).then_inc(S("rest_filled"), 16)
            for u in range(6):
                wait_lo(sp, NE - 1, u)
            for i in range(NT):
                M = rows_of(i)
                sp.dma_start(x1c[i][0:M], x1_dram[i * P:i * P + M, :]).then_inc(S(f"x1_back{i}"), 16)
            sp.dma_start(bc_g2, ln2_g[0:1, :].to_broadcast((P, D))).then_inc(S("ln2_rows"), 16)
            sp.dma_start(bc_b2, ln2_b[0:1, :].to_broadcast((P, D))).then_inc(S("ln2_rows"), 16)
            for i in range(NT):
                sp.wait_ge(S("out_ready"), i + 1)
                sp.dma_start(ys if i == NT - 1 else yp[i * P:(i + 1) * P, :], x1c[i][0:rows_of(i)]
                             ).then_inc(S("stored"), 16)
            sp.wait_ge(S("stored"), 16 * NT)

        @block.gpsimd
        def _(pool):
            own = Tally(S("pool_setup"))

            def then(ins):
                pool.wait_ge(own.sem, own(ins))
            own(pool.memset(ident, 0.0))
            own(pool.memset(ones, 1.0))
            own(pool.memset(TRI[:, :, :], 1.0))
            own(pool.memset(wpool, 0.0))
            own(pool.memset(epsc, EPS))
            for a, hist in ((aP, HA), (bP, HB), (cP, HC)):
                own(pool.memset(a[:, :, 0:hist], 0.0))
            own(pool.iota(tpos, [[1, HB + 1]], base=1, channel_multiplier=0, allow_small_or_imprecise_dtypes=True))
            pool.wait_ge(own.sem, own.n)
            pool.affine_select(out=ident, in_=ident, compare_op=ALU.not_equal, fill=1.0, base=0,
                               pattern=[[-1, P]], channel_multiplier=1).then_inc(S("ident_ready"), 1)
            pool.affine_select(out=TRI[:, 0, :], in_=TRI[:, 0, :], compare_op=ALU.is_gt, fill=0.0, base=0,
                               pattern=[[1, P]], channel_multiplier=-1).then_inc(S("ident_ready"), 1)
            for g in range(4):
                h = 64 * (g % 2)
                pool.dma_start(wpool[h:h + 64, (g // 2) * P + h:(g // 2) * P + h + 64], w_pool[0, g]
                               ).then_inc(S("wpool_in"), 16)
            pool.dma_start(wrt.rearrange("p (k c) -> p k c", k=KD)[:, :, 0:NG],
                           w_rg[0].rearrange("(k p) c -> p k c", p=P)).then_inc(S("router_in"), 16)
            pool.dma_start(wrt.rearrange("p (k c) -> p k c", k=KD)[:, :, NG:NG + NE],
                           w_re[0].rearrange("(k p) c -> p k c", p=P)).then_inc(S("router_in"), 16)
            pool.dma_start(brt[:, 0:NG], b_rg[0:1, :].to_broadcast((P, NG))).then_inc(S("router_in"), 16)
            pool.dma_start(brt[:, NG:], b_re[0:1, :].to_broadcast((P, NE))).then_inc(S("router_in"), 16)

            def win_lo(n, q):
                pool.wait_ge(S("win_hi"), n + 1)
                pool.tensor_tensor(win[:, q, 1], wraw[q].rearrange("p (k m) -> p k m", k=KD),
                                   win[:, q, 0].bitcast(F32), ALU.subtract).then_inc(S("win_lo"), 1)

            def gate_mul(m, n, P_, S_, c, hist):
                pool.wait_ge(S("projected"), n)
                pool.wait_ge(S("history_in"), 4)
                p_, s_ = P_[:, ds(c, 1), hist:hist + SEQ], S_[:, ds(c, 1), :, hist:hist + DECT]
                pool.tensor_tensor(p_, p_, gs[:, 0:SEQ].rearrange("p (a t) -> p a t", a=1), ALU.mult
                                   ).then_inc(S("gate_mul"), 1)
                pool.tensor_tensor(s_, s_, gs[:, SEQ:].rearrange("p (a b t) -> p a b t", a=1, b=DECB), ALU.mult
                                   ).then_inc(S("gate_mul"), 1)

            win_lo(0, 0)
            win_lo(1, 1)
            with pool.Fori(0, CA) as c:
                win_lo(2 * c + 2, 0)
                gate_mul(c, 2 * c + 2, aP, aS, c, HA)
                win_lo(2 * c + 3, 1)
            win_lo(N_U + 2, 0)
            win_lo(N_U + 3, 1)

            t = [mix[:, 5 + i, :] for i in range(2)]
            u = [RAW[:, OFF_STAGE + i * DECB * LBS:OFF_STAGE + (i + 1) * DECB * LBS]
                 .rearrange("p (b t) -> p b t", b=DECB) for i in range(2)]
            sums = Tally(S("window_sums"))

            def window_sums(c):
                for i in range(2 * c + 2):
                    lo, step = 2 ** (i + 1) - 1, 2 ** i
                    a = bP[:, c] if i == 0 else t[(i - 1) % 2]
                    b = bS[:, c] if i == 0 else u[(i - 1) % 2]
                    if i > 0:
                        pool.wait_ge(sums.sem, sums.n)
                    sums(pool.tensor_tensor(t[i % 2][:, lo:LB], a[:, lo:LB], a[:, lo - step:LB - step], ALU.add))
                    sums(pool.tensor_tensor(u[i % 2][:, :, lo:LBS], b[:, :, lo:LBS], b[:, :, lo - step:LBS - step],
                                            ALU.add))
            pool.wait_ge(S("projected"), N_U + 2)
            window_sums(0)
            win_lo(N_C + 2, 0)
            gate_mul(3, N_C + 2, cP, cS, 0, HC)
            win_lo(N_C + 3, 1)
            pool.wait_ge(S("pooled"), 6)
            window_sums(1)
            with pool.Fori(1, CC) as c:
                win_lo(N_C + 2 * c + 2, 0)
                gate_mul(3 + c, N_C + 2 * c + 2, cP, cS, c, HC)
                win_lo(N_C + 2 * c + 3, 1)
            win_lo(NCH - 1, 0)

            def mix_lo(i):
                M = rows_of(i)
                pool.wait_ge(S("mix_hi"), i + 1)
                pool.tensor_tensor(mhl[:, i % 2, 1, :, 0:M], mix[:, :, i * P:i * P + M],
                                   mhl[:, i % 2, 0, :, 0:M].bitcast(F32), ALU.subtract).then_inc(S("mix_lo"), 1)
            mix_lo(0)
            mix_lo(1)
            pool.wait_ge(S("ln1_rows"), 48)
            for i in range(NT):
                M = rows_of(i)
                r = trow[(i + 2) % 3][0:M]
                if i + 2 < NT:
                    mix_lo(i + 2)
                pool.wait_ge(S("x1_normed"), i + 1)
                pool.tensor_tensor(r, r, bc_g1[0:M], ALU.mult).then_inc(S("x1_scaled"), 1)
                pool.wait_ge(S("x1_scaled"), i + 1)
                pool.tensor_tensor(r, r, bc_b1[0:M], ALU.add).then_inc(S("x1_ready"), 1)

            own2 = Tally(S("route_consts"))
            pool.wait_ge(S("mix_lo"), NT)
            for dst, n, base, step, mult in ((ig, P, 0, 1, 0), (it, NTAB, 0, 1, 0), (tokid, NT, 0, P, 1),
                                             (dsc, EPG, EPG, -1, 0)):
                own2(pool.iota(dst, [[step, n]], base=base, channel_multiplier=mult,
                               allow_small_or_imprecise_dtypes=True))

            pool.memset(carrier[:, 0:1], 0.0).then_inc(S("y_free"), 1)
            pool.memset(carrier[:, 1:2], 0.0).then_inc(S("y_copied"), 1)

            def gather(t):
                pool.tensor_copy(idxc, table[:, ds(t, 1)]).then_inc(S("index_copied"), 1)
                pool.wait_ge(S("index_copied"), t + 1)
                pool.tensor_tensor(carrier[:, 0:1], epsc, epsc, ALU.add)
                pool.indirect_dma_start(xg, None, x1_dram, bass.IndirectOffsetOnAxis(ap=idxc, axis=0)
                                        ).then_inc(S("rows_in"), 16)

            def lo_unit(e, u):
                h, l = unit_parts(u)
                pool.wait_ge(S("unit_hi"), 6 * e + u + 1)
                pool.tensor_tensor(l, unit_raw(u), h.bitcast(F32), ALU.subtract).then_inc(S("unit_lo_pool"), 1)

            pool.wait_ge(S("table_ready"), 1)
            pool.wait_ge(S("x1_stored"), 16 * NT)
            gather(0)
            for u in LO_POOL:
                lo_unit(0, u)
            pool.wait_ge(S("xe_turned"), 1)
            gather(1)

            def tile(t, e, last):
                if last:
                    lo_unit(e + 1, LO_POOL[0])
                pool.wait_ge(S("xe_turned"), t + 2)
                gather(t + 2)
                pool.wait_ge(S("y_copied"), t + 2)
                pool.dma_start(y_dram[ds(t * P, P), :], yrow).then_inc(S("y_stored"), 16)
                if last:
                    lo_unit(e + 1, LO_POOL[1])
                pool.wait_ge(S("y_stored"), 16 * t + 16)
                pool.tensor_tensor(carrier[:, 1:2], epsc, epsc, ALU.add).then_inc(S("y_free"), 1)
            expert_tiles(pool, tile)

            _first, last = first_last(pool, NE - 1)
            rest = pool.value_load(NTI[0:1, 2 * NE:], min_val=1, max_val=YT)
            pool.wait_ge(S("rest_filled"), 16 * rest)
            pool.wait_ge(S("y_stored"), 16 * last + 16)
            pool.wait_ge(S("rows_in"), 16 * last + 48)
            pool.tensor_tensor(carrier[:, 2:3], epsc, epsc, ALU.add)

            def gather_y(i):
                M = rows_of(i)
                if i >= 4:
                    pool.wait_ge(S("out_weighed"), i - 3)
                for c in range(2):
                    pool.indirect_dma_start(yg[2 * (i % 4) + c][0:M], None, y_dram,
                                            bass.IndirectOffsetOnAxis(ap=slot[0:M, c, i:i + 1], axis=0)
                                            ).then_inc(S(f"y_back{i % 4}"), 16)
            for i in range(4):
                gather_y(i)
            pool.wait_ge(S("ln2_rows"), 32)
            for i in range(NT):
                M = rows_of(i)
                pool.wait_ge(S("out_scaled"), i + 1)
                pool.tensor_tensor(x1c[i][0:M], x1c[i][0:M], bc_b2[0:M], ALU.add).then_inc(S("out_ready"), 1)
                if i + 4 < NT:
                    gather_y(i + 4)

        @block.scalar
        def _(act):
            act.dma_start(vec_rows[0:TAPS * CA, 0, :], conv_a_w[0].rearrange("t (c p) -> (t c) p", p=P)
                          ).then_inc(S("vectors_in"), 16)
            at = 0
            for src in (b_in, conv_a_b, ln_a_g, ln_a_b, pool_scale):
                n = src.shape[1] // P
                act.dma_start(vec_rows[at:at + n, 1, :], src[0].rearrange("(c p) -> c p", p=P)
                              ).then_inc(S("vectors_in"), 16)
                at += n
            act.dma_start(vec_rows[at:at + 3 * CC, 1, :], conv_c_w[0].rearrange("t (c p) -> (t c) p", p=P)
                          ).then_inc(S("vectors_in"), 16)
            for h in range(2):
                act.dma_start(hist_a[0:120, h, :], st_a[0, 4 * h:4 * h + 4].rearrange("b t c -> (b t) c")
                              ).then_inc(S("states_in"), 16)
            act.dma_start(hist_b[0:120, :], st_b[0].rearrange("b t c -> (b t) c")).then_inc(S("states_in"), 16)
            act.dma_start(hist_c[0:DECB * HC, :], st_c[0].rearrange("b t c -> (b t) c")).then_inc(S("states_in"), 16)

            def win_hi(n, q):
                act.wait_ge(S(f"win_raw{q}"), 16 * ((n - q) // 2 + 1) if isinstance(n, int) else (n - q) * 8 + 16)
                act.activation(win[:, q, 0], wraw[q].rearrange("p (k m) -> p k m", k=KD), ACT.Copy
                               ).then_inc(S("win_hi"), 1)
            win_hi(0, 0)
            win_hi(1, 1)

            def x_hi(i, q, M):
                act.wait_ge(S("x_turned"), i + 1)
                for h in range(2):
                    act.activation(xT[:, 0, 4 * h:4 * h + 4, ds(i * P, M)],
                                   bank(2 * q + h).rearrange("p (k m) -> p k m", k=4)[:, :, 0:M], ACT.Copy
                                   ).then_inc(S("x_hi"), 1)
            with act.Fori(0, 4) as i:
                for q in range(2):
                    x_hi(2 * i + q, q, P)
            x_hi(NT - 1, 0, NS)

            def evacuate(n, q, col_, func, dst_p, dst_s):
                act.wait_ge(S("multiplied"), n + 1)
                b = pcol(col_)
                for g in range(2):
                    act.activation(dst_p(g * GRP, GRP), bank(3 * q + g, GRP), func, bias=b)
                act.activation(dst_p(2 * GRP, LASTP), bank(3 * q + 2, LASTP), func, bias=b)
                act.activation(dst_s, bank(3 * q + 2, GRP)[:, LASTP:].rearrange("p (b t) -> p b t", b=DECB),
                               func, bias=b).then_inc(S("projected"), 1)

            def to_ext(n, q, col_, P_, S_, c, hist, func=ACT.Identity):
                evacuate(n, q, col_, func,
                         lambda a, m: P_[:, ds(c, 1), hist + a:hist + a + m].rearrange("p a t -> p (a t)"),
                         S_[:, ds(c, 1), :, hist:hist + DECT].rearrange("p a b t -> p (a b) t"))

            def to_gs(n, q, col_, func):
                evacuate(n, q, col_, func, lambda a, m: gs[:, a:a + m],
                         gs[:, SEQ:].rearrange("p (b t) -> p b t", b=DECB))

            act.wait_ge(S("vectors_ready"), 2)
            def gated(c):
                to_ext(2 * c, 0, BLK_VAL + c, aP, aS, c, HA)
                win_hi(2 * c + 2, 0)
                if not (isinstance(c, int) and c == 0):
                    act.wait_ge(S("gate_mul"), 2 * c)
                to_gs(2 * c + 1, 1, BLK_GATE + c, ACT.Sigmoid)
                win_hi(2 * c + 3, 1)
            gated(0)
            with act.Fori(1, CA) as c:
                gated(c)
            for q in range(CB):
                to_ext(N_U + q, q, BLK_U + q, bP, bS, q, HB)
                win_hi(N_U + q + 2, q)
            with act.Fori(0, CC) as c:
                to_ext(N_C + 2 * c, 0, BLK_CG + c, cP, cS, c, HC)
                win_hi(N_C + 2 * c + 2, 0)
                act.wait_ge(S("gate_mul"), 2 * (CA + c))
                to_gs(N_C + 2 * c + 1, 1, BLK_H + c, ACT.Identity)
                win_hi(N_C + 2 * c + 3, 1)

            def square(g):
                act.wait_ge(S("centred"), 3 * (g + 1))
                act.activation(squares, mix[:, 0:CA, g * GRP:(g + 1) * GRP], ACT.Square).then_inc(S("squared"), 1)
            square(0)
            act.wait_ge(S("gate_mul"), 2 * (CA + CC))
            to_gs(N_BG, 0, BLK_BG, ACT.Identity)
            win_hi(NCH - 1, 0)

            act.wait_ge(S("pooled"), 12)
            for j in range(3):
                rows = min(PER_A, DECB - PER_A * j) * LAS
                misc_ready(act, f"a{j}")
                act.activation(out_a[0:rows, j, :], bank(MB[f"a{j}"], WA, rows), ACT.Copy).then_inc(S("state_out_a"), 1)
            for c in range(CB):
                for g in range(3):
                    misc_ready(act, f"p{c}{g}")
                    act.activation(mix[:, CA + c, g * GRP:(g + 1) * GRP], bank(MB[f"p{c}{g}"], GRP), ACT.Copy,
                                   scale=pcol(COL_PS + c)).then_inc(S("pool_out"), 1)
            for g in range(3):
                misc_ready(act, f"v{g}")
                if g > 0:
                    act.wait_ge(S("ln_a_norm"), 3 * g)
                act.activation(stdev, bank(MB[f"v{g}"], GRP), ACT.Sqrt, bias=epsc, scale=1.0 / WA
                               ).then_inc(S("stdev_a"), 1)
                if g < 2:
                    square(g + 1)
            act.wait_ge(S("short_done"), 2)
            to_gs(N_BG + 1, 1, BLK_BG + 1, ACT.Identity)
            act.wait_ge(S("ln_a_norm"), 9)
            for c in range(CA):
                act.activation(mix[:, c], mix[:, c], ACT.Silu, bias=pcol(COL_B + c), scale=pcol(COL_G + c)
                               ).then_inc(S("swished"), 1)
            act.wait_ge(S("win_lo"), NCH - 1)
            nb0 = min(PER_B, DECB)
            for name, dst, rows, n in (("b0", out_b[:, 0, :], nb0 * LBS, WB), ("b1", out_b[:, 1, :], (DECB - nb0) * LBS, WB),
                                       ("b2", out_b[:, 2, :], HB, WB), ("c0", out_c, DECB * LCS, WC),
                                       ("c1", out_cp, HC, WC), ("a3", out_ap, HA, WA)):
                misc_ready(act, name)
                act.activation(dst[0:rows], bank(MB[name], n, rows), ACT.Copy).then_inc(S("state_out_bc"), 1)
            act.wait_ge(S("short_done"), 4)
            to_gs(N_BG + 2, 0, BLK_BG + 2, ACT.Identity)

            def wo_hi(u):
                act.wait_ge(S(f"wo_raw{u}"), 16)
                act.activation(unit_parts(u)[0], unit_raw(u), ACT.Copy).then_inc(S("wo_hi"), 1)

            def mix_hi(i):
                M = rows_of(i)
                act.activation(mhl[:, i % 2, 0, :, 0:M], mix[:, :, i * P:i * P + M], ACT.Copy).then_inc(S("mix_hi"), 1)
            act.wait_ge(S("pool_out"), 6)
            act.wait_ge(S("swished"), CA)
            wo_hi(0)
            act.wait_ge(S("short_done"), 2 * CC)
            mix_hi(0)
            wo_hi(1)
            wo_hi(2)
            mix_hi(1)
            wo_hi(3)

            def turn_copy(i):
                M = rows_of(i)
                act.wait_ge(S("x1_turned"), i + 1)
                act.wait_ge(S("routed"), i)
                act.activation(x1T[:, :, 0:M], PS[:, 4:6, :].rearrange("p b (k m) -> p (b k) m", k=4)[:, :, 0:M],
                               ACT.Copy).then_inc(S("x1T_ready"), 1)
            for i in range(NT):
                M = rows_of(i)
                if i + 2 < NT:
                    act.wait_ge(S("out_multiplied"), i + 1)
                    mix_hi(i + 2)
                act.wait_ge(S("stats1"), i + 1)
                act.activation(sd[i % 2][0:M], mv[i % 2][0:M, 1:2], ACT.Sqrt, bias=epsc[0:M]).then_inc(S("stdev1"), 1)
                act.wait_ge(S("norm1"), 2 * (i + 1))
                r = trow[(i + 2) % 3][0:M]
                act.activation(r, r, ACT.Identity, bias=nmr[i % 2][0:M], scale=rstd[i % 2][0:M]
                               ).then_inc(S("x1_normed"), 1)
                if i > 0:
                    turn_copy(i - 1)

            def hi_unit(e, u):
                h, _l = unit_parts(u)
                act.wait_ge(S(f"unit_raw{u}"), (32 if u < 4 else 16) * (e + 1))
                act.activation(h, unit_raw(u), ACT.Copy).then_inc(S("unit_hi"), 1)
            turn_copy(NT - 1)
            act.wait_ge(S("out_multiplied"), NT)
            for u in (0, 1):
                hi_unit(0, u)
            act.wait_ge(S("logits_less"), 1)
            act.activation(g36[4], g36[3], ACT.Exp).then_inc(S("exps"), 1)
            act.wait_ge(S("logits_less"), 2)
            act.activation(g9[5], g9[4], ACT.Exp).then_inc(S("exps"), 1)
            for u in (2, 3, 4, 5):
                hi_unit(0, u)

            def xe_hi(t):
                act.wait_ge(S("xe_turned"), t + 1)
                act.activation(xe[:, 0], PS[:, 2:4, :].rearrange("p b (k m) -> p (b k) m", k=4), ACT.Copy
                               ).then_inc(S("xe_hi"), 1)
            xe_hi(0)

            def tile(t, e, last):
                act.wait_ge(S("first_half"), t + 1)
                act.activation(hid[:, 0:256], bank(0)[:, 0:256], ACT.Silu).then_inc(S("silu_done"), 1)
                act.wait_ge(S("hid_turned"), 2 * t + 1)
                act.activation(he[:, 0, 0:2, :], bank(4)[:, 0:256].rearrange("p (k m) -> p k m", k=2), ACT.Copy
                               ).then_inc(S("he_hi"), 1)
                if last:
                    for u in (0, 1):
                        act.wait_ge(S("unit_used"), 6 * t + u + 1)
                        hi_unit(e + 1, u)
                act.wait_ge(S("unit_used"), 6 * t + 4)
                act.activation(hid[:, 256:512], bank(1)[:, 0:256], ACT.Silu).then_inc(S("silu_done"), 1)
                if last:
                    hi_unit(e + 1, 2)
                act.wait_ge(S("hid_turned"), 2 * t + 2)
                act.activation(he[:, 0, 2:4, :], bank(4)[:, 256:512].rearrange("p (k m) -> p k m", k=2), ACT.Copy
                               ).then_inc(S("he_hi"), 1)
                xe_hi(t + 1)
                if last:
                    hi_unit(e + 1, 3)
                act.wait_ge(S("unit_used"), 6 * t + 6)
                act.wait_ge(S("y_free"), t + 1)
                act.activation(yrow, PS[:, 5:7, :].rearrange("p b n -> p (b n)"), ACT.Copy).then_inc(S("y_copied"), 1)
                if last:
                    for u in (4, 5):
                        hi_unit(e + 1, u)
            expert_tiles(act, tile)

            for i in range(NT):
                M = rows_of(i)
                act.wait_ge(S(f"x1_back{i}"), 16)
                act.activation(x1c[i][0:M], x1c[i][0:M], ACT.Copy, scale=ALPHA).then_inc(S("x1_alpha"), 1)
            for i in range(NT):
                M = rows_of(i)
                act.wait_ge(S("stats2"), i + 1)
                act.activation(sd[i % 2][0:M], mv[i % 2][0:M, 1:2], ACT.Sqrt, bias=epsc[0:M]).then_inc(S("stdev2"), 1)
                act.wait_ge(S("norm2"), 2 * (i + 1))
                act.activation(x1c[i][0:M], x1c[i][0:M], ACT.Identity, bias=nmr[i % 2][0:M], scale=rstd[i % 2][0:M]
                               ).then_inc(S("out_normed"), 1)

        @block.vector
        def _(dve):
            dve.wait_ge(S("small_turned"), 2)
            dve.tensor_copy(pcA, bank(4, TAPS * CA)).then_inc(S("vectors_ready"), 1)
            dve.tensor_copy(pcB, bank(4)[:, P:P + 37]).then_inc(S("vectors_ready"), 1)
            dve.wait_ge(S("small_turned"), 6)
            for h in range(2):
                dve.tensor_copy(aS[:, :, 4 * h:4 * h + 4, 0:HA],
                                bank(5 + h, 360).rearrange("p (c b t) -> p c b t", c=CA, b=4)
                                ).then_inc(S("history_in"), 1)
            dve.tensor_copy(bS[:, :, :, 0:HB], bank(7, 240).rearrange("p (c b t) -> p c b t", c=CB, b=DECB)
                            ).then_inc(S("history_in"), 1)
            dve.tensor_copy(cS[:, :, :, 0:HC], bank(7)[:, 256:304].rearrange("p (c b t) -> p c b t", c=CC, b=DECB)
                            ).then_inc(S("history_in"), 1)
            own = Tally(S("dve_setup"))
            for c in range(CB):
                for h in range(2):
                    w = 2.0 ** (2 * c + h + 1)
                    own(dve.memset(winv[64 * h:64 * h + 64, c:c + 1], 1.0 / w))
                    own(dve.memset(wmin[64 * h:64 * h + 64, c:c + 1], w))
            dve.wait_ge(own.sem, own.n)
            dve.wait_ge(S("ident_ready"), 2)
            rc = rcnt.rearrange("p (c t) -> p c t", c=CB)
            for c in range(CB):
                own(dve.tensor_scalar(rc[:, c], tpos, wmin[:, c:c + 1], None, ALU.min))
            dve.wait_ge(own.sem, own.n)
            own(dve.reciprocal(rcnt, rcnt))

            def x_lo(i, q, M):
                for h in range(2):
                    dve.wait_ge(S("x_hi"), 2 * i + h + 1)
                    dve.tensor_tensor(xT[:, 1, 4 * h:4 * h + 4, ds(i * P, M)],
                                      bank(2 * q + h).rearrange("p (k m) -> p k m", k=4)[:, :, 0:M],
                                      xT[:, 0, 4 * h:4 * h + 4, ds(i * P, M)].bitcast(F32), ALU.subtract
                                      ).then_inc(S("x_lo"), 1)
            with dve.Fori(0, 4) as i:
                for q in range(2):
                    x_lo(2 * i + q, q, P)
            x_lo(NT - 1, 0, NS)

            def taps(c, n, w_of, bias, P_, S_, out, sem, base):
                for j in range(n):
                    parts = [(out[:, ds(c, 1), h * 512:(h + 1) * 512],
                              P_[:, ds(c, 1), j + h * 512:j + (h + 1) * 512]) for h in range(2)]
                    parts.append((out[:, ds(c, 1), SEQ:].rearrange("p a (b t) -> p (a b) t", b=DECB),
                                  S_[:, ds(c, 1), :, j:j + DECT].rearrange("p a b t -> p (a b) t")))
                    for h, (o, a) in enumerate(parts):
                        if j == 0 and bias is not None:
                            ins = dve.tensor_scalar(o, a, w_of(j), bias, ALU.mult, ALU.add)
                        elif j == 0:
                            ins = dve.tensor_scalar(o, a, w_of(j), None, ALU.mult)
                        else:
                            dve.wait_ge(sem, base + 3 * (j - 1) + h + 1)
                            ins = dve.scalar_tensor_tensor(o, a, w_of(j), o, ALU.mult, ALU.add)
                        ins.then_inc(sem, 1)

            def conv_a(c):
                dve.wait_ge(S("gate_mul"), 2 * (c + 1))
                taps(c, TAPS, lambda j: pcA[:, ds(j * CA + c, 1)], pcol(COL_CB + c), aP, aS, mix,
                     S("conv_taps"), 3 * TAPS * c)

            def pool_d(c):
                dve.wait_ge(S("window_sums"), 4 if c == 0 else 12)
                m, base = mix[:, CA + c], 6 * c
                tt = [mix[:, 5 + i, :] for i in range(2)]
                uu = [RAW[:, OFF_STAGE + i * DECB * LBS:OFF_STAGE + (i + 1) * DECB * LBS]
                      .rearrange("p (b t) -> p b t", b=DECB) for i in range(2)]
                for h in range(2):
                    r = slice(64 * h, 64 * h + 64)
                    w = winv[r, c:c + 1]
                    dve.scalar_tensor_tensor(m[r, HB + 1:SEQ], tt[h][r, 2 * HB + 1:LB], w, bP[r, c, 2 * HB + 1:LB],
                                             ALU.mult, ALU.subtract).then_inc(S("pooled"), 1)
                    dve.scalar_tensor_tensor(m[r, SEQ:].rearrange("p (b t) -> p b t", b=DECB), uu[h][r, :, HB:], w,
                                             bS[r, c, :, HB:], ALU.mult, ALU.subtract).then_inc(S("pooled"), 1)
                    dve.tensor_tensor(m[r, 0:HB + 1], tt[h][r, HB:2 * HB + 1], rc[r, c], ALU.mult
                                      ).then_inc(S("pool_head"), 1)
                    dve.wait_ge(S("pool_head"), 2 * c + h + 1)
                    dve.tensor_tensor(m[r, 0:HB + 1], m[r, 0:HB + 1], bP[r, c, HB:2 * HB + 1], ALU.subtract
                                      ).then_inc(S("pooled"), 1)

            with dve.Fori(0, 2) as c:
                conv_a(c)
            dve.wait_ge(own.sem, own.n)
            pool_d(0)
            conv_a(2)
            pool_d(1)

            for g in range(3):
                misc_ready(dve, f"m{g}")
                for c in range(CA):
                    m = mix[:, c, g * GRP:(g + 1) * GRP]
                    dve.scalar_tensor_tensor(m, bank(MB[f"m{g}"], GRP), -1.0 / WA, m, ALU.mult, ALU.add
                                             ).then_inc(S("centred"), 1)

            def short_conv(c):
                dve.wait_ge(S("gate_mul"), 2 * (CA + c + 1))
                taps(c, 3, lambda j: pcol(COL_CW + j * CC + c), None, cP, cS, mix[:, 5:8], S("short_conv"), 9 * c)

            def norm_a(g):
                dve.wait_ge(S("stdev_a"), g + 1)
                dve.reciprocal(stdev, stdev).then_inc(S("rstd_a"), 1)
                dve.wait_ge(S("rstd_a"), g + 1)
                for c in range(CA):
                    m = mix[:, c, g * GRP:(g + 1) * GRP]
                    dve.tensor_tensor(m, m, stdev, ALU.mult).then_inc(S("ln_a_norm"), 1)

            def short_mul(c):
                dve.wait_ge(S("projected"), N_BG + c + 1)
                for h in range(2):
                    m = mix[:, 5 + c, h * 528:(h + 1) * 528]
                    dve.tensor_tensor(m, m, gs[:, h * 528:(h + 1) * 528], ALU.mult).then_inc(S("short_done"), 1)
            short_conv(0)
            dve.wait_ge(S("short_conv"), 9)
            short_mul(0)
            for g in range(3):
                norm_a(g)
                if g > 0:
                    short_conv(g)
            dve.wait_ge(S("short_conv"), 27)
            short_mul(1)
            short_mul(2)

            for u in range(4):
                dve.wait_ge(S("wo_hi"), u + 1)
                dve.tensor_tensor(unit_parts(u)[1], unit_raw(u), unit_parts(u)[0].bitcast(F32), ALU.subtract
                                  ).then_inc(S("wo_lo"), 1)
            dve.wait_ge(S("pool_out"), 6)
            dve.memset(L[:, NT - 1, :], 0.0).then_inc(S("logits_cleared"), 1)
            dve.wait_ge(S("ln1_rows"), 48)

            def stats(i, r, sem):
                q, M = i % 2, rows_of(i)
                for h in range(2):
                    dve.bn_stats(bn[q][0:M, h], r[:, h * 512:(h + 1) * 512]).then_inc(S("bn_steps" + sem), 1)
                dve.wait_ge(S("bn_steps" + sem), 2 * (i + 1))
                dve.bn_aggr(mv[q][0:M], bn[q][0:M].rearrange("p h s -> p (h s)")).then_inc(S("stats" + sem), 1)

            def scales(i, sem):
                q, M = i % 2, rows_of(i)
                dve.wait_ge(S("stdev" + sem), i + 1)
                dve.reciprocal(rstd[q][0:M], sd[q][0:M]).then_inc(S("norm" + sem), 1)
                dve.wait_ge(S("norm" + sem), 2 * i + 1)
                dve.scalar_tensor_tensor(nmr[q][0:M], mv[q][0:M, 0:1], -1.0, rstd[q][0:M], ALU.mult, ALU.mult
                                         ).then_inc(S("norm" + sem), 1)

            def logits(i):
                M = rows_of(i)
                dve.wait_ge(S("routed"), i + 1)
                dve.tensor_tensor(L[0:M, i, :], bank(6, NG + NE, M), brt[0:M], ALU.add).then_inc(S("logits"), 1)

            for i in range(NT):
                M = rows_of(i)
                r = trow[(i + 2) % 3][0:M]
                dve.wait_ge(S(f"x_again{i % 3}"), 16 * (i // 3 + 1))
                dve.scalar_tensor_tensor(r, r, ALPHA, bc_bo[0:M], ALU.mult, ALU.add).then_inc(S("residual"), 1)
                dve.wait_ge(S("residual"), i + 1)
                dve.wait_ge(S("out_multiplied"), i + 1)
                for h in range(2):
                    dve.tensor_tensor(r[:, h * 512:(h + 1) * 512], bank(2 * (i % 2) + h, rows=M),
                                      r[:, h * 512:(h + 1) * 512], ALU.add).then_inc(S("out_taken"), 1)
                dve.wait_ge(S("out_taken"), 2 * (i + 1))
                if i >= 2:
                    dve.wait_ge(S("x1_normed"), i - 1)
                stats(i, r, "1")
                scales(i, "1")
                if i > 1:
                    logits(i - 2)
            logits(NT - 2)
            logits(NT - 1)

            step = Tally(S("route_steps"))

            def do(ins):
                dve.wait_ge(step.sem, step(ins))

            def over(a, n):
                return a.rearrange("p (i o) -> p i o", o=1).to_broadcast((P, NT, n))

            def last4(a):
                return a.rearrange("p (o c) -> p o c", o=1).to_broadcast((P, NT, NG))
            dve.wait_ge(S("logits"), NT)
            dve.wait_ge(S("logits_cleared"), 1)
            dve.wait_ge(S("route_consts"), 4)
            G, E = L[:, :, 0:NG], L[:, :, NG:]

            def first_max(v, top, eq, ohv, m):
                do(dve.tensor_reduce(top, v, AX, ALU.max))
                do(dve.tensor_tensor(eq, v, over(top, NG), ALU.is_equal))
                do(dve.tensor_tensor(eq, eq, last4(dsc), ALU.mult))
                do(dve.tensor_reduce(m, eq, AX, ALU.max))
                do(dve.tensor_tensor(ohv, last4(dsc), over(m, NG), ALU.is_equal))
            gmax, gsum, gp, v1, dv, ex, v2, m9, w1, rs = g9
            eq, ohg, oh1, gd, ge, esel, oh2, esel2 = g36
            OH1, OH2, prod, prod2 = g144
            first_max(G, gmax, eq, ohg, m9)
            dve.tensor_tensor(gd, G, over(gmax, NG), ALU.subtract).then_inc(S("logits_less"), 1)
            do(dve.tensor_tensor(prod, E.rearrange("p i (g j) -> p i g j", g=NG),
                                 ohg.rearrange("p i (g o) -> p i g o", o=1).to_broadcast((P, NT, NG, EPG)), ALU.mult))
            do(dve.tensor_reduce(esel, prod.rearrange("p i g j -> p i j g"), AX, ALU.add))
            first_max(esel, v1, eq, oh1, m9)
            do(dve.scalar_tensor_tensor(esel2, oh1, -3.0e38, esel, ALU.mult, ALU.add))
            first_max(esel2, v2, eq, oh2, m9)
            dve.tensor_tensor(dv, v2, v1, ALU.subtract).then_inc(S("logits_less"), 1)
            for OH, oh in ((OH1, oh1), (OH2, oh2)):
                do(dve.tensor_tensor(OH, ohg.rearrange("p i (g o) -> p i g o", o=1).to_broadcast((P, NT, NG, EPG)),
                                     oh.rearrange("p i (o j) -> p i o j", o=1).to_broadcast((P, NT, NG, EPG)), ALU.mult))
            flat = [o.rearrange("p i g j -> p i (g j)") for o in (OH1, OH2)]
            do(dve.tensor_tensor(Mb, flat[0], flat[1], ALU.add))
            for lo in range(NS, P, 32):
                dve.memset(Mb[lo:lo + 32, NT - 1, :], 0.0).then_inc(S("choices"), 1)
            dve.wait_ge(S("exps"), 2)
            do(dve.tensor_reduce(gsum, ge, AX, ALU.add))
            do(dve.reciprocal(gp, gsum))
            do(dve.tensor_scalar(rs, ex, 1.0, None, ALU.add))
            do(dve.reciprocal(rs, rs))
            do(dve.tensor_tensor(wgt[:, 0], rs, gp, ALU.mult))
            do(dve.tensor_tensor(wgt[:, 1], wgt[:, 0], ex, ALU.mult))
            dve.wait_ge(S("ranked"), 1)
            counts_ps = bank(7)[:, NT * NE:(NT + 1) * NE]
            ciI, ci2I = ci.bitcast(I32), ci2.bitcast(I32)
            do(dve.tensor_scalar(ciI, counts_ps, float(P - 1), None, ALU.add))
            do(dve.tensor_scalar(ci2I, ciI, 7, None, ALU.logical_shift_right))
            do(dve.tensor_scalar(ntf, ci2I, 1.0, None, ALU.max))
            do(dve.tensor_tensor_scan(inc, ones[:, 0:NE], ntf, 0.0, ALU.mult, ALU.add))
            do(dve.tensor_tensor(exc, inc, ntf, ALU.subtract))
            dve.tensor_copy(NTI[:, 0:NE], exc).then_inc(S("counts_ready"), 1)
            dve.tensor_scalar(NTI[:, NE:2 * NE], inc, -1.0, None, ALU.add).then_inc(S("counts_ready"), 1)
            dve.tensor_scalar(NTI[:, 2 * NE:], inc[:, NE - 1:], -1.0, float(YT), ALU.mult, ALU.add
                              ).then_inc(S("counts_ready"), 1)
            rank, base, ri, rhi, rhf, rlo, rlf, tcol, slf = r18
            rk = bank(7, NT * NE).rearrange("p (i e) -> p i e", i=NT)
            pe3 = [x.rearrange("p i g j -> p i (g j)") for x in (prod, prod2)]
            for c in range(2):
                do(dve.tensor_tensor(pe3[0], rk, flat[c], ALU.mult))
                do(dve.tensor_reduce(rank[:, c], pe3[0], AX, ALU.add))
                do(dve.tensor_tensor(pe3[1], flat[c], exc.rearrange("p (o e) -> p o e", o=1).to_broadcast((P, NT, NE)),
                                     ALU.mult))
                do(dve.tensor_reduce(base[:, c], pe3[1], AX, ALU.add))
            rI, rhI, rlI = ri.bitcast(I32), rhi.bitcast(I32), rlo.bitcast(I32)
            do(dve.tensor_copy(rI, rank))
            do(dve.tensor_scalar(rhI, rI, 7, None, ALU.logical_shift_right))
            do(dve.tensor_scalar(rlI, rI, P - 1, None, ALU.bitwise_and))
            do(dve.tensor_tensor(tcol, base, rhI, ALU.add))
            do(dve.tensor_copy(rlf, rlI))
            do(dve.scalar_tensor_tensor(slf, tcol, float(P), rlf, ALU.mult, ALU.add))
            do(dve.tensor_copy(slot, slf))
            for n in range(2 * NT):
                c, i = n % 2, n // 2
                if n >= 2:
                    dve.wait_ge(S("table_sum"), n - 1)
                dve.tensor_scalar(ohp[c], ig, rlf[:, c, i:i + 1], None, ALU.is_equal).then_inc(S("one_hot"), 1)
                dve.tensor_scalar(oht[c], it, tcol[:, c, i:i + 1], tokid[:, i:i + 1], ALU.is_equal, ALU.mult
                                  ).then_inc(S("one_hot"), 1)
            dve.wait_ge(S("table_sum"), 2 * NT)
            dve.tensor_copy(table, bank(6, NTAB)).then_inc(S("table_ready"), 1)

            def lo_unit(e, u):
                h, l = unit_parts(u)
                dve.wait_ge(S("unit_hi"), 6 * e + u + 1)
                dve.tensor_tensor(l, unit_raw(u), h.bitcast(F32), ALU.subtract).then_inc(S("unit_lo_dve"), 1)
            for u in LO_DVE:
                lo_unit(0, u)

            def xe_lo(t):
                dve.wait_ge(S("xe_hi"), t + 1)
                dve.tensor_tensor(xe[:, 1], PS[:, 2:4, :].rearrange("p b (k m) -> p (b k) m", k=4),
                                  xe[:, 0].bitcast(F32), ALU.subtract).then_inc(S("xe_lo"), 1)
            xe_lo(0)

            def tile(t, e, last):
                def hidden(h):
                    dve.wait_ge(S("silu_done"), 2 * t + h + 1)
                    v = hid[:, h * 256:(h + 1) * 256]
                    dve.tensor_tensor(v, v, bank(h)[:, 256:512], ALU.mult).then_inc(S("hidden"), 1)

                def he_lo(h):
                    dve.wait_ge(S("he_hi"), 2 * t + h + 1)
                    dve.tensor_tensor(he[:, 1, 2 * h:2 * h + 2, :],
                                      bank(4)[:, h * 256:(h + 1) * 256].rearrange("p (k m) -> p k m", k=2),
                                      he[:, 0, 2 * h:2 * h + 2, :].bitcast(F32), ALU.subtract).then_inc(S("he_lo"), 1)
                hidden(0)
                he_lo(0)
                if last:
                    lo_unit(e + 1, 0)
                hidden(1)
                if last:
                    lo_unit(e + 1, 2)
                he_lo(1)
                xe_lo(t + 1)
                if last:
                    for u in (3, 4):
                        lo_unit(e + 1, u)
            expert_tiles(dve, tile)

            dve.wait_ge(S("ln2_rows"), 32)

            def finish(i):
                M = rows_of(i)
                dve.wait_ge(S("out_normed"), i + 1)
                dve.tensor_tensor(x1c[i][0:M], x1c[i][0:M], bc_g2[0:M], ALU.mult).then_inc(S("out_scaled"), 1)
            for i in range(NT):
                M = rows_of(i)
                o = x1c[i][0:M]
                dve.wait_ge(S("x1_alpha"), i + 1)
                dve.wait_ge(S(f"y_back{i % 4}"), 32 * (i // 4 + 1))
                for c in range(2):
                    dve.scalar_tensor_tensor(o, yg[2 * (i % 4) + c][0:M], wgt[0:M, c, i:i + 1], o, ALU.mult, ALU.add
                                             ).then_inc(S("weigh_steps" if c == 0 else "out_weighed"), 1)
                    dve.wait_ge(S("weigh_steps" if c == 0 else "out_weighed"), i + 1)
                if i >= 2:
                    dve.wait_ge(S("out_normed"), i - 1)
                stats(i, o, "2")
                if i > 0:
                    finish(i - 1)
                scales(i, "2")
            finish(NT - 1)

        @block.tensor
        def _(pe):
            def turn(out, in_, n):
                return pe.transpose(out, in_, ident[0:n, 0:n])

            pe.wait_ge(S("ident_ready"), 2)
            pe.wait_ge(S("vectors_in"), 16 * 7)
            turn(bank(4, TAPS * CA), vec_rows[0:TAPS * CA, 0, :], TAPS * CA).then_inc(S("small_turned"), 1)
            turn(bank(4)[:, P:P + 37], vec_rows[0:37, 1, :], 37).then_inc(S("small_turned"), 1)
            pe.wait_ge(S("states_in"), 16 * 4)
            for h in range(2):
                for c in range(CA):
                    mm = turn(bank(5 + h)[:, c * 120:(c + 1) * 120], hist_a[0:120, h, c * P:(c + 1) * P], 120)
                mm.then_inc(S("small_turned"), 1)
            for c in range(CB):
                mm = turn(bank(7)[:, c * 120:(c + 1) * 120], hist_b[0:120, c * P:(c + 1) * P], 120)
            mm.then_inc(S("small_turned"), 1)
            for c in range(CC):
                mm = turn(bank(7)[:, 256 + c * 16:256 + (c + 1) * 16], hist_c[0:16, c * P:(c + 1) * P], 16)
            mm.then_inc(S("small_turned"), 1)

            def turn_x(i, q, M, n):
                pe.wait_ge(S(f"x_rows{q}"), n)
                for c in range(KD):
                    mm = turn(bank(2 * q + c // 4)[:, (c % 4) * P:(c % 4) * P + M],
                              xrow[q][0:M, c * P:(c + 1) * P], M)
                mm.then_inc(S("x_turned"), 1)
            for q in range(2):
                turn_x(q, q, P, 16)
            with pe.Fori(1, 4) as i:
                for q in range(2):
                    pe.wait_ge(S("x_lo"), 4 * i + 2 * q - 2)
                    turn_x(2 * i + q, q, P, 16 * i + 16)
            pe.wait_ge(S("x_lo"), 2 * (NT - 2))
            turn_x(NT - 1, 0, NS, 16 * 5)

            def project(n, q):
                pe.wait_ge(S("win_lo"), n + 1)
                for c in range(KD):
                    for ws, xs_ in ((0, 0), (0, 1), (1, 0)):
                        for g in range(3):
                            mm = pe.matmul(bank(3 * q + g, GRP), win[:, q, ws, c, :],
                                           xT[:, xs_, c, g * GRP:(g + 1) * GRP],
                                           start=(c == 0 and ws + xs_ == 0), stop=(c == KD - 1 and ws == 1))
                mm.then_inc(S("multiplied"), 1)

            pe.wait_ge(S("x_lo"), 2 * NT)
            pe.wait_ge(S("history_in"), 4)
            project(0, 0)
            project(1, 1)
            with pe.Fori(1, (N_BG) // 2) as i:
                for q in range(2):
                    pe.wait_ge(S("projected"), 2 * i + q - 1)
                    project(2 * i + q, q)

            def job(name):
                j = job_no[name]
                if j >= 2:
                    _n, s_, v = jobs[j - 2]
                    pe.wait_ge(S(s_), v)
                return bank(MB[name])

            def summed(name, src):
                o = job(name)
                for c in range(CA):
                    mm = pe.matmul(o[:, 0:GRP], ones, src(c), start=(c == 0), stop=(c == CA - 1))
                mm.then_inc(S("misc_done"), 1)

            pe.wait_ge(S("conv_taps"), 3 * TAPS * CA)
            for g in range(3):
                summed(f"m{g}", lambda c: mix[:, c, g * GRP:(g + 1) * GRP])
            pe.wait_ge(S("projected"), N_BG - 1)
            project(N_BG, 0)

            def turn_rows(name, src, chunks):
                o = job(name)
                for c in range(chunks):
                    r = src(c)
                    mm = turn(o[0:r.shape[1], c * P:(c + 1) * P], r, P)
                mm.then_inc(S("misc_done"), 1)

            def sequences(S_, c, b0, n):
                return S_[:, c, b0:b0 + n, :].rearrange("p b t -> p (b t)")
            for j in range(3):
                turn_rows(f"a{j}", lambda c: sequences(aS, c, PER_A * j, min(PER_A, DECB - PER_A * j)), CA)
            pe.wait_ge(S("pooled"), 12)
            pe.wait_ge(S("wpool_in"), 64)
            for c in range(CB):
                for g in range(3):
                    pe.matmul(job(f"p{c}{g}")[:, 0:GRP], wpool[:, c * P:(c + 1) * P],
                              mix[:, CA + c, g * GRP:(g + 1) * GRP], start=True, stop=True).then_inc(S("misc_done"), 1)
            for g in range(3):
                pe.wait_ge(S("squared"), g + 1)
                summed(f"v{g}", lambda c: squares[:, c])
            pe.wait_ge(S("projected"), N_BG)
            project(N_BG + 1, 1)
            pe.wait_ge(S("gate_mul"), 2 * (CA + CC))
            nb0 = min(PER_B, DECB)
            turn_rows("b0", lambda c: sequences(bS, c, 0, nb0), CB)
            turn_rows("b1", lambda c: sequences(bS, c, nb0, DECB - nb0), CB)
            turn_rows("b2", lambda c: bP[:, c, SEQ:], CB)
            turn_rows("c0", lambda c: sequences(cS, c, 0, DECB), CC)
            turn_rows("c1", lambda c: cP[:, c, SEQ:], CC)
            turn_rows("a3", lambda c: aP[:, c, SEQ:], CA)
            pe.wait_ge(S("projected"), N_BG + 1)
            project(N_BG + 2, 0)

            pe.wait_ge(S("projected"), NCH)

            def route(i):
                M = rows_of(i)
                pe.wait_ge(S("x1T_ready"), i + 1)
                pe.wait_ge(S("router_in"), 64)
                if i > 0:
                    pe.wait_ge(S("logits"), i)
                for c in range(KD):
                    mm = pe.matmul(bank(6, NG + NE, M), x1T[:, c, 0:M], wrt[:, c * 20:(c + 1) * 20],
                                   start=(c == 0), stop=(c == KD - 1))
                mm.then_inc(S("routed"), 1)

            def turn_x1(i):
                M = rows_of(i)
                pe.wait_ge(S("x1_ready"), i + 1)
                if i > 0:
                    pe.wait_ge(S("x1T_ready"), i)
                for c in range(KD):
                    mm = turn(bank(4 + c // 4)[:, (c % 4) * P:(c % 4) * P + M],
                              trow[(i + 2) % 3][0:M, c * P:(c + 1) * P], M)
                mm.then_inc(S("x1_turned"), 1)

            for i in range(NT):
                M = rows_of(i)
                pe.wait_ge(S("mix_lo"), i + 1)
                if i >= 2:
                    pe.wait_ge(S("out_taken"), 2 * (i - 1))
                for c in range(KD):
                    if i == 0 and c % 2 == 0:
                        pe.wait_ge(S("wo_lo"), c // 2 + 1)
                    for ms, ws in ((0, 0), (0, 1), (1, 0)):
                        for h in range(2):
                            mm = pe.matmul(bank(2 * (i % 2) + h, rows=M), mhl[:, i % 2, ms, c, 0:M],
                                           wo[:, ws, c, h * 512:(h + 1) * 512],
                                           start=(c == 0 and ms + ws == 0), stop=(c == KD - 1 and ms == 1))
                mm.then_inc(S("out_multiplied"), 1)
                if i > 1:
                    route(i - 2)
                if i > 0:
                    turn_x1(i - 1)
            route(NT - 2)
            turn_x1(NT - 1)
            route(NT - 1)

            pe.wait_ge(S("choices"), 3)
            rk = bank(7, NT * NE)
            mflat = Mb.rearrange("p i e -> p (i e)")
            pe.matmul(rk, TRI[:, 0, :], mflat, start=True, stop=False, skip_group_check=True)
            for i in range(NT - 1):
                n = NT - 1 - i
                pe.matmul(rk.rearrange("p (i e) -> p i e", i=NT)[:, i + 1:, :], TRI[:, 1, :],
                          Mb[:, i:i + 1, :].to_broadcast((P, n, NE)), start=False, stop=(i == NT - 2),
                          skip_group_check=True)
            for i in range(NT):
                mm = pe.matmul(bank(7)[:, NT * NE:(NT + 1) * NE], TRI[:, 1, :], Mb[:, i, :],
                               start=(i == 0), stop=(i == NT - 1), skip_group_check=True)
            mm.then_inc(S("ranked"), 1)
            for n in range(2 * NT):
                c, i = n % 2, n // 2
                M = rows_of(i)
                pe.wait_ge(S("one_hot"), 2 * n + 2)
                pe.matmul(bank(6, NTAB), ohp[c][0:M], oht[c][0:M], start=(n == 0), stop=(n == 2 * NT - 1)
                          ).then_inc(S("table_sum"), 1)

            def turn_xe(t):
                pe.wait_ge(S("rows_in"), 16 * t + 16)
                for c in range(KD):
                    mm = turn(bank(2 + c // 4)[:, (c % 4) * P:(c % 4 + 1) * P], xg[:, c:D:KD], P)
                mm.then_inc(S("xe_turned"), 1)

            def turn_hid(h):
                for c in (2 * h, 2 * h + 1):
                    mm = turn(bank(4)[:, c * P:(c + 1) * P], hid[:, c * P:(c + 1) * P], P)
                mm.then_inc(S("hid_turned"), 1)

            turn_xe(0)

            def tile(t, e, last):
                pe.wait_ge(S("xe_lo"), t + 1)
                for h in range(2):
                    for c in range(KD):
                        if h == 0 and c % 2 == 0:
                            wait_lo(pe, e, c // 2)
                        for xs_, ws in ((0, 0), (0, 1), (1, 0)):
                            w = wo[:, ws, c, :].rearrange("p (s f) -> p s f", s=2)[:, :, h * 256:(h + 1) * 256]
                            mm = pe.matmul(bank(h), xe[:, xs_, c, :], w, start=(c == 0 and xs_ + ws == 0),
                                           stop=(c == KD - 1 and xs_ == 1))
                        if h == 0 and c == KD - 1:
                            mm.then_inc(S("first_half"), 1)
                        if h == 1 and c % 2 == 1:
                            mm.then_inc(S("unit_used"), 1)
                        if h == 1 and c == 3:
                            pe.wait_ge(S("hidden"), 2 * t + 1)
                            turn_hid(0)
                turn_xe(t + 1)
                pe.wait_ge(S("he_lo"), 2 * t + 1)
                pe.wait_ge(S("y_copied"), t + 1)
                wait_lo(pe, e, 4)
                for c in range(KF):
                    for hs, ws in ((0, 0), (0, 1), (1, 0)):
                        for h in range(2):
                            mm = pe.matmul(bank(5 + h), he[:, hs, c, :], wd[:, ws, c, h * 512:(h + 1) * 512],
                                           start=(c == 0 and hs + ws == 0), stop=(c == KF - 1 and hs == 1))
                    if c % 2 == 1:
                        mm.then_inc(S("unit_used"), 1)
                    if c == 0:
                        pe.wait_ge(S("hidden"), 2 * t + 2)
                        turn_hid(1)
                    if c == 1:
                        pe.wait_ge(S("he_lo"), 2 * t + 2)
                        wait_lo(pe, e, 5)
            expert_tiles(pe, tile)


_INS = ["x_prompt", "x_sample", "state_conv_a", "state_pool_b", "state_conv_c", "w_in", "b_in", "conv_a_w",
        "conv_a_b", "ln_a_g", "ln_a_b", "w_pool", "pool_scale", "conv_c_w", "w_out", "b_out", "ln1_g", "ln1_b",
        "w_router_group", "b_router_group", "w_router_expert", "b_router_expert", "w_gate", "w_up", "w_down",
        "ln2_g", "ln2_b"]
_OUTS = [(1, SEQ, D), (DECB, DECT, D), (1, 1, HA, WA), (1, DECB, HA, WA), (1, 1, HB, WB), (1, DECB, HB, WB),
         (1, 1, HC, WC), (1, DECB, HC, WC)]


def kernel(**inputs):
    import numpy as _np
    import concourse.bacc as _bacc
    from concourse import mybir as _mybir
    from concourse.bass_utils import run_bass_kernel_spmd as _run

    nc = _bacc.Bacc("TRN2", target_bir_lowering=False, num_devices=1)
    arrays, args = {}, []
    for name in _INS:
        a = _np.ascontiguousarray(inputs[name])
        arrays[f"in_{name}"] = a
        args.append(nc.dram_tensor(f"in_{name}", a.shape, _mybir.dt.from_np(a.dtype), kind="ExternalInput").ap())
    for i, shape in enumerate(_OUTS):
        args.append(nc.dram_tensor(f"out_{i}", shape, _mybir.dt.float32, kind="ExternalOutput").ap())
    build(nc, *args)
    r = _run(nc, [arrays], core_ids=[0])
    return tuple(r.results[0][f"out_{i}"] for i in range(len(_OUTS)))
```

```python
from contextlib import ExitStack

import concourse.bass as bass
from concourse import mybir

F32 = mybir.dt.float32
F32R = mybir.dt.float32r
BF16 = mybir.dt.bfloat16
I32 = mybir.dt.int32
U32 = mybir.dt.uint32
ALU = mybir.AluOpType
ACT = mybir.ActivationFunctionType
AX = mybir.AxisListType.X
ds = bass.ds

P = 128
D = 1024
SEQ, DECB, DECT = 1024, 8, 4
NS = DECB * DECT
TOK = SEQ + NS
KD = D // P
NT = (TOK + P - 1) // P
GRP = TOK // 3
LASTP = SEQ - 2 * GRP
WA, WB, WC = 384, 256, 384
CA, CB, CC = WA // P, WB // P, WC // P
D_IN = 2 * WA + WB + 3 * WC
NCH = D_IN // P
TAPS, HA = 31, 30
HB = 15
HC = 2
NG, EPG = 4, 4
NE = NG * EPG
F = 512
KF = F // P
EPS = 1e-5
ALPHA = 2.0 ** 0.25
MAXT = (2 * TOK + NE * (P - 1)) // P
NTAB = MAXT + 2
YT = MAXT + 1

BLK_VAL, BLK_GATE, BLK_U, BLK_BG, BLK_CG, BLK_H = 0, CA, 2 * CA, 2 * CA + CB, 2 * CA + CB + CC, 2 * CA + CB + 2 * CC
ORDER = ([b for c in range(CA) for b in (BLK_VAL + c, BLK_GATE + c)] + [BLK_U, BLK_U + 1]
         + [b for c in range(CC) for b in (BLK_CG + c, BLK_H + c)] + [BLK_BG + c for c in range(CC)])

LA, LAS = HA + SEQ, HA + DECT
EXTA = CA * (LA + DECB * LAS)
LB, LBS = HB + SEQ, HB + DECT
LC, LCS = HC + SEQ, HC + DECT
OFF_B = 2 * 2 * D
OFF_C = OFF_B + CB * (LB + DECB * LBS)
OFF_STAGE = OFF_C + CC * (LC + DECB * LCS)
OFF_BC = 4 * 2 * D
RAWW = OFF_BC + 3 * D


class Tally:

    def __init__(self, sem):
        self.sem, self.n = sem, 0

    def __call__(self, ins, by=1):
        ins.then_inc(self.sem, by)
        self.n = self.n + by
        return self.n


def build(nc, x_prompt, x_sample, st_a, st_b, st_c, w_in, b_in, conv_a_w, conv_a_b, ln_a_g, ln_a_b,
          w_pool, pool_scale, conv_c_w, w_out, b_out, ln1_g, ln1_b, w_rg, b_rg, w_re, b_re,
          w_gate, w_up, w_down, ln2_g, ln2_b, y_p, y_s, na_p, na_s, nb_p, nb_s, nc_p, nc_s):
    x1_dram = nc.dram_tensor("x1_rows", (TOK, D), F32).ap()
    y_dram = nc.dram_tensor("expert_rows", (YT * P, D), F32).ap()
    xp, xs = x_prompt[0], x_sample.rearrange("b t d -> (b t) d")
    yp, ys = y_p[0], y_s.rearrange("b t d -> (b t) d")

    with ExitStack() as ctx:
        def sb(name, shape, dt):
            return ctx.enter_context(nc.sbuf_tensor(name, shape, dt))

        sems = {}

        def S(name):
            if name not in sems:
                sems[name] = ctx.enter_context(nc.semaphore(name))
            return sems[name]

        BIG = sb("BIG", [P, 2 * KD * TOK], F32R)
        WD = sb("WD", [P, 2 * KF * D], F32R)
        TH = sb("TH", [P, 3 * D], F32R)
        RAW = sb("RAW", [P, RAWW], F32)
        MIX = sb("MIX", [P, KD * TOK], F32)
        F2 = sb("F2", [P, 4 * TOK], F32)
        C = sb("C", [P, 912], F32)
        TRI = sb("TRI", [P, 2, P], BF16)
        NTI = sb("NTI", [P, 2 * NE + 1], I32)
        PS = ctx.enter_context(nc.psum_tensor("PS", [P, 8, 512], F32))

        col = [0]

        def const(n):
            a = col[0]
            col[0] += n
            assert col[0] <= 912
            return C[:, a:a + n]

        ident, ones = const(P), const(P)
        wpool = const(CB * P)
        pcA, pcB = const(TAPS * CA), const(37)
        wrt = const(KD * (NG + NE))
        brt = const(NG + NE)
        winv, wmin, tpos, rcnt = const(CB), const(CB), const(HB + 1), const(CB * (HB + 1))
        epsc, zc = const(1), const(1)

        def pcol(block):
            return pcB[:, block:block + 1] if isinstance(block, int) else pcB[:, ds(block, 1)]

        COL_CB, COL_G, COL_B, COL_PS, COL_CW = NCH, NCH + 3, NCH + 6, NCH + 9, NCH + 11

        xT = BIG[:, :].rearrange("p (s k t) -> p s k t", s=2, k=KD)
        wo = (BIG[:, :].rearrange("p (s x) -> p s x", s=2)[:, :, 0:KD * D].rearrange("p s (k n) -> p s k n", k=KD))
        win = WD[:, 0:4 * D].rearrange("p (q s k m) -> p q s k m", q=2, s=2, k=KD)
        mhl = WD[:, 4 * D:8 * D].rearrange("p (q s k m) -> p q s k m", q=2, s=2, k=KD)
        wd = WD[:, :].rearrange("p (s k n) -> p s k n", s=2, k=KF)
        xe = TH[:, 0:2 * D].rearrange("p (s k m) -> p s k m", s=2, k=KD)
        he = TH[:, 2 * D:3 * D].rearrange("p (s k m) -> p s k m", s=2, k=KF)

        def ext(off, chunks, length, slen):
            a = RAW[:, off:off + chunks * length].rearrange("p (c t) -> p c t", c=chunks)
            o = off + chunks * length
            b = RAW[:, o:o + chunks * DECB * slen].rearrange("p (c b t) -> p c b t", c=chunks, b=DECB)
            return a, b

        aP, aS = ext(0, CA, LA, LAS)
        bP, bS = ext(OFF_B, CB, LB, LBS)
        cP, cS = ext(OFF_C, CC, LC, LCS)
        unit = [RAW[:, u * 2 * D:(u + 1) * 2 * D] if u < 4 else MIX[:, (u - 4) * 2 * D:(u - 3) * 2 * D]
                for u in range(6)]
        bc_g1, bc_b1, bc_bo = (RAW[:, OFF_BC + i * D:OFF_BC + (i + 1) * D] for i in range(3))
        mix = MIX[:, :].rearrange("p (c t) -> p c t", c=KD)
        gs = F2[:, 0:TOK]
        xrow = ([F2[:, 0:D], F2[:, TOK:TOK + D]] + [MIX[:, (2 + i) * D:(3 + i) * D] for i in range(NT - 3)]
                + [RAW[:, OFF_STAGE:OFF_STAGE + D]])
        wraw = [F2[:, 2 * TOK:2 * TOK + D], F2[:, 2 * TOK + D:2 * TOK + 2 * D]]
        trow = [F2[:, i * TOK:i * TOK + D] for i in range(3)]
        x1T = F2[:, 3 * TOK:3 * TOK + D].rearrange("p (k m) -> p k m", k=KD)
        moff = [4 * D]

        def mx(n):
            a = moff[0]
            moff[0] += n
            assert moff[0] <= KD * TOK
            return MIX[:, a:a + n]

        def bank(b, n=512, rows=P):
            return PS[0:rows, b, 0:n]

        def rows_of(i):
            return P if i < NT - 1 else TOK - (NT - 1) * P


        rc = rcnt.rearrange("p (c t) -> p c t", c=CB)

        L = wpool[:, 0:NT * 20].rearrange("p (i c) -> p i c", i=NT)
        bn = [wpool[:, 180 + 18 * q:192 + 18 * q].rearrange("p (h s) -> p h s", h=2) for q in range(2)]
        mv = [wpool[:, 192 + 18 * q:194 + 18 * q] for q in range(2)]
        sd = [wpool[:, 194 + 18 * q:195 + 18 * q] for q in range(2)]
        rstd = [wpool[:, 195 + 18 * q:196 + 18 * q] for q in range(2)]
        nmr = [wpool[:, 196 + 18 * q:197 + 18 * q] for q in range(2)]

        ig = mx(P)
        it = mx(NTAB)
        tokid = mx(NT + 1)
        dsc = mx(EPG)
        iint = mx(P).bitcast(I32)
        g9 = [mx(NT) for _ in range(10)]
        g36 = [mx(NT * NG).rearrange("p (i c) -> p i c", i=NT) for _ in range(8)]
        OHB = mx(2 * NT * NE).rearrange("p (k i e) -> p k i e", k=2, i=NT)
        OH1, OH2 = (OHB[:, k].rearrange("p i (g j) -> p i g j", g=NG) for k in range(2))
        prod = mx(NT * NE).rearrange("p (i g j) -> p i g j", i=NT, g=NG)
        Mb = mx(NT * NE // 2).bitcast(BF16).rearrange("p (i e) -> p i e", i=NT)
        ntf, inc, exc, ci, ci2 = (mx(NE) for _ in range(5))
        r18 = [mx(2 * NT).rearrange("p (k i) -> p k i", k=2) for _ in range(6)]
        wgt = mx(2 * NT).rearrange("p (k i) -> p k i", k=2)
        slot = mx(2 * NT).bitcast(U32).rearrange("p (k i) -> p k i", k=2)
        ohp = RAW[:, OFF_BC:OFF_BC + NT * P].bitcast(BF16).rearrange("p (k i m) -> p k i m", k=2, i=NT)
        oht = RAW[:, OFF_BC + NT * P:OFF_BC + NT * (P + 2 * NTAB)].bitcast(BF16
                  ).rearrange("p (k i h m) -> p k i h m", k=2, i=NT, h=2)
        ohe = RAW[:, OFF_BC + NT * (P + 2 * NTAB):OFF_BC + NT * (P + 4 * NTAB)
                  ].rearrange("p (k i m) -> p k i m", k=2, i=NT)
        tabf = mx(2 * NTAB)
        table = mx(NTAB).bitcast(U32)
        idxc = mx(1).bitcast(U32)
        diag = mx(4 * P).rearrange("p (q c m) -> p q c m", q=2, c=2)
        carrier = mx(4)
        xg, yrow, hid = F2[:, 0:D], F2[:, TOK:TOK + D], F2[:, 2 * TOK:2 * TOK + F]
        x1c = [RAW[:, i * D:(i + 1) * D] for i in range(8)] + [RAW[:, OFF_BC:OFF_BC + D]]
        bc_g2, bc_b2 = RAW[:, OFF_BC + D:OFF_BC + 2 * D], RAW[:, OFF_BC + 2 * D:OFF_BC + 3 * D]
        yg = [MIX[:, i * D:(i + 1) * D] for i in range(4)] + [F2[:, i * TOK:i * TOK + D] for i in range(4)]

        out_a = RAW[:, OFF_STAGE:OFF_STAGE + 3 * WA].rearrange("p (s n) -> p s n", s=3)
        out_b = RAW[:, OFF_B:OFF_B + 3 * WB].rearrange("p (s n) -> p s n", s=3)
        out_ap, out_c = (RAW[:, OFF_B + 3 * WB + i * WA:OFF_B + 3 * WB + (i + 1) * WA] for i in range(2))
        out_cp = RAW[:, OFF_STAGE + 3 * WA:OFF_STAGE + 4 * WA]
        stdev = [F2[:, 2 * TOK + g * GRP:2 * TOK + (g + 1) * GRP] for g in range(3)]
        wsum_p = [mix[:, 5 + i] for i in range(2)]
        wsum_s = [RAW[:, OFF_STAGE + i * DECB * LBS:OFF_STAGE + (i + 1) * DECB * LBS]
                  .rearrange("p (b t) -> p b t", b=DECB) for i in range(2)]
        prods = [(mix[:, 5 + c], F2[:, TOK:2 * TOK], mix[:, 6 + c] if c < CC - 1 else gs) for c in range(CC)]
        PER_A, PER_B = P // LAS, P // LBS
        squares = F2[:, 3 * TOK:4 * TOK].rearrange("p (c t) -> p c t", c=CA)

        vec_rows = MIX[:, 0:2 * P].rearrange("p (s n) -> p s n", s=2)
        hist_a = MIX[:, 2 * P:2 * P + 2 * WA].rearrange("p (s n) -> p s n", s=2)
        hist_b = MIX[:, 2 * P + 2 * WA:2 * P + 2 * WA + WB]
        hist_c = MIX[:, 2 * P + 2 * WA + WB:2 * P + 3 * WA + WB]

        jobs = ([(f"a{j}", "state_out_a", j + 1) for j in range(3)]
                + [(n, "state_out_bc", j + 2) for j, n in enumerate(("b01", "b2", "a3"))]
                + [(f"p{c}{g}", "pool_out", 3 * c + g + 1) for c in range(CB) for g in range(3)]
                + [(f"m{g}", "centred", 3 * (g + 1)) for g in range(3)]
                + [(n, "state_out_bc", j + 5) for j, n in enumerate(("c0", "c1"))]
                + [(f"v{g}", "stdev_a", g + 1) for g in range(3)])
        job_no = {name: j for j, (name, _, _) in enumerate(jobs)}
        MB = {name: 6 + j % 2 for j, (name, _, _) in enumerate(jobs)}

        def misc_ready(eng, name):
            eng.wait_ge(S("misc_done"), job_no[name] + 1)

        def taps(eng, c, n, w_of, bias, P_, S_, out, sem, base):
            for j in range(n):
                parts = [(out[:, ds(c, 1), h * 512:(h + 1) * 512],
                          P_[:, ds(c, 1), j + h * 512:j + (h + 1) * 512]) for h in range(2)]
                parts.append((out[:, ds(c, 1), SEQ:].rearrange("p a (b t) -> p (a b) t", b=DECB),
                              S_[:, ds(c, 1), :, j:j + DECT].rearrange("p a b t -> p (a b) t")))
                for h, (o, a) in enumerate(parts):
                    if j == 0 and bias is not None:
                        ins = eng.tensor_scalar(o, a, w_of(j), bias, ALU.mult, ALU.add)
                    elif j == 0:
                        ins = eng.tensor_scalar(o, a, w_of(j), None, ALU.mult)
                    else:
                        eng.wait_ge(sem, base + 3 * (j - 1) + h + 1)
                        ins = eng.scalar_tensor_tensor(o, a, w_of(j), o, ALU.mult, ALU.add)
                    ins.then_inc(sem, 1)

        N_U, N_C, N_BG = 2 * CA, 2 * CA + CB, 2 * CA + CB + 2 * CC

        LO_MOST, LO_REST = (0, 2, 3, 4), (1, 5)

        DVE_WEIGHS = 3
        POOL_SCALES = (1, 4)
        DVE_SCALES = tuple(i for i in range(NT) if i not in POOL_SCALES)

        def lo_sem(u):
            return S("unit_lo_most" if u in LO_MOST else "unit_lo_rest")

        def wait_lo(eng, e, u):
            units = LO_MOST if u in LO_MOST else LO_REST
            eng.wait_ge(lo_sem(u), len(units) * e + units.index(u) + 1)

        def lo_unit(eng, e, u):
            h, l = unit_parts(u)
            eng.wait_ge(S("unit_hi"), 6 * e + u + 1)
            eng.tensor_tensor(l, unit_raw(u), h.bitcast(F32), ALU.subtract).then_inc(lo_sem(u), 1)

        def unit_parts(u):
            if u < 4:
                return wo[:, 0, 2 * u:2 * u + 2, :], wo[:, 1, 2 * u:2 * u + 2, :]
            return wd[:, 0, 2 * (u - 4):2 * (u - 3), :], wd[:, 1, 2 * (u - 4):2 * (u - 3), :]

        def unit_raw(u):
            return unit[u].rearrange("p (k n) -> p k n", k=2)

        def first_last(eng, e):
            return [eng.value_load(NTI[0:1, ds(e + h * NE, 1)], min_val=0, max_val=MAXT - 1) for h in range(2)]

        def expert_tiles(eng, tile):
            eng.wait_ge(S("counts_ready"), 3)

            def one(e, splits):
                first, last = first_last(eng, e)
                with eng.If(first < last):
                    with eng.Fori(first, last) as t:
                        tile(t, e, False)
                tile(last, e, splits)
            with eng.Fori(0, NE - 1) as e:
                one(e, True)
            one(NE - 1, False)

        def load_unit(sp, e, u):
            if u < 4:
                for h, w in enumerate((w_gate, w_up)):
                    src = w[0, ds(e, 1)].rearrange("a (p k) f -> p (a k) f", p=P)[:, 2 * u:2 * u + 2, :]
                    sp.dma_start(unit_raw(u)[:, :, h * F:(h + 1) * F], src).then_inc(S(f"unit_raw{u}"), 16)
            else:
                v = u - 4
                src = w_down[0, ds(e, 1), v * 2 * P:(v + 1) * 2 * P, :].rearrange("a (k p) n -> p (a k) n", p=P)
                sp.dma_start(unit_raw(u), src).then_inc(S(f"unit_raw{u}"), 16)

        def mix_lo(eng, i):
            M = rows_of(i)
            eng.wait_ge(S("mix_hi"), i + 1)
            eng.tensor_tensor(mhl[:, i % 2, 1, :, 0:M], mix[:, :, i * P:i * P + M],
                               mhl[:, i % 2, 0, :, 0:M].bitcast(F32), ALU.subtract).then_inc(S("mix_lo"), 1)

        def wo_lo(eng, u):
            eng.wait_ge(S("wo_hi"), u + 1)
            eng.tensor_tensor(unit_parts(u)[1], unit_raw(u), unit_parts(u)[0].bitcast(F32), ALU.subtract
                              ).then_inc(S("wo_lo"), 1)

        block = ctx.enter_context(nc.Block())

        @block.sync
        def _(sp):
            def load_x(i):
                sp.dma_start(xrow[i][0:rows_of(i)], xs if i == NT - 1 else xp[i * P:(i + 1) * P, :]
                             ).then_inc(S(f"x_rows{i}"), 16)

            def load_w(n, q, block_):
                src = w_in[0, :, ds(block_ * P, P)].rearrange("(k p) m -> p k m", p=P)
                sp.dma_start(wraw[q].rearrange("p (k m) -> p k m", k=KD), src).then_inc(S(f"win_raw{q}"), 16)

            load_w(0, 0, ORDER[0])
            for i in range(NT):
                load_x(i)
            load_w(1, 1, ORDER[1])
            sp.dma_start(vec_rows[0:TAPS * CA, 0, :], conv_a_w[0].rearrange("t (c p) -> (t c) p", p=P)
                         ).then_inc(S("vectors_in"), 16)
            at = 0
            for src in (b_in, conv_a_b, ln_a_g, ln_a_b, pool_scale):
                n = src.shape[1] // P
                sp.dma_start(vec_rows[at:at + n, 1, :], src[0].rearrange("(c p) -> c p", p=P)
                             ).then_inc(S("vectors_in"), 16)
                at += n
            sp.dma_start(vec_rows[at:at + 3 * CC, 1, :], conv_c_w[0].rearrange("t (c p) -> (t c) p", p=P)
                         ).then_inc(S("vectors_in"), 16)
            for h in range(2):
                sp.dma_start(hist_a[0:120, h, :], st_a[0, 4 * h:4 * h + 4].rearrange("b t c -> (b t) c")
                             ).then_inc(S("states_in"), 16)
            sp.dma_start(hist_b[0:120, :], st_b[0].rearrange("b t c -> (b t) c")).then_inc(S("states_in"), 16)
            sp.dma_start(hist_c[0:DECB * HC, :], st_c[0].rearrange("b t c -> (b t) c")).then_inc(S("states_in"), 16)

            def win_pair(n, b0, b1):
                for q, b in enumerate((b0, b1)):
                    sp.wait_ge(S("win_lo"), n + q - 1)
                    load_w(n + q, q, b)
            with sp.Fori(1, CA) as c:
                win_pair(2 * c, BLK_VAL + c, BLK_GATE + c)
            win_pair(N_U, BLK_U, BLK_U + 1)
            with sp.Fori(0, CC) as c:
                win_pair(N_C + 2 * c, BLK_CG + c, BLK_H + c)
            win_pair(N_BG, BLK_BG, BLK_BG + 1)
            sp.wait_ge(S("win_lo"), N_BG + 1)
            load_w(N_BG + 2, 0, BLK_BG + 2)

            sp.wait_ge(S("state_out_a"), 3)
            for b in range(DECB):
                r = (b % PER_A) * LAS + DECT
                sp.dma_start(na_s[0, b], out_a[r:r + HA, b // PER_A, :]).then_inc(S("state_stored_a"), 16)

            def load_wo(u):
                sp.dma_start(unit_raw(u), w_out[0, u * 2 * P:(u + 1) * 2 * P, :].rearrange("(k p) n -> p k n", p=P)
                             ).then_inc(S(f"wo_raw{u}"), 16)

            def load_t(i):
                sp.dma_start(trow[(i + 2) % 3][0:rows_of(i)], xs if i == NT - 1 else xp[i * P:(i + 1) * P, :]
                             ).then_inc(S(f"x_again{i % 3}"), 16)
            sp.wait_ge(S("state_out_bc"), 4)
            for b in range(DECB):
                r = (b % PER_B) * LBS + DECT
                sp.dma_start(nb_s[0, b], out_b[r:r + HB, b // PER_B, :]).then_inc(S("state_stored_bc"), 16)
            sp.dma_start(nb_p[0, 0], out_b[0:HB, 2, :]).then_inc(S("state_stored_bc"), 16)
            sp.dma_start(na_p[0, 0], out_ap[0:HA, :]).then_inc(S("state_stored_bc"), 16)
            sp.wait_ge(S("conv_taps"), 3 * TAPS * CA)
            load_wo(0)
            load_wo(1)
            sp.wait_ge(S("state_out_bc"), 6)
            for b in range(DECB):
                r = b * LCS + DECT
                sp.dma_start(nc_s[0, b], out_c[r:r + HC, :]).then_inc(S("state_stored_bc"), 16)
            sp.dma_start(nc_p[0, 0], out_cp[0:HC, :]).then_inc(S("state_stored_bc"), 16)
            sp.wait_ge(S("tap_products"), CC)
            sp.wait_ge(S("state_stored_bc"), 16 * (2 * DECB + 3))
            load_wo(2)
            load_wo(3)
            sp.wait_ge(S("win_lo"), NCH)
            sp.wait_ge(S("state_stored_a"), 16 * DECB)
            for dst, src in ((bc_bo, b_out), (bc_g1, ln1_g), (bc_b1, ln1_b)):
                sp.dma_start(dst, src[0:1, :].to_broadcast((P, D))).then_inc(S("ln1_rows"), 16)
            misc_ready(sp, "v2")
            sp.wait_ge(S("ln_a_norm"), 9)
            load_t(0)
            sp.wait_ge(S("short_conv"), 2 * CC)
            load_t(1)
            load_t(2)
            for i in range(NT):
                sp.wait_ge(S("x1_ready"), i + 1)
                M = rows_of(i)
                sp.dma_start(x1_dram[i * P:i * P + M, :], trow[(i + 2) % 3][0:M]).then_inc(S("x1_stored"), 16)
                if i + 3 < NT:
                    sp.wait_ge(S("x1_stored"), 16 * (i + 1))
                    sp.wait_ge(S("x1_turned"), i + 1)
                    load_t(i + 3)
                if i == 0:
                    for u in range(4):
                        sp.wait_ge(S("wo_lo"), u + 1)
                        load_unit(sp, 0, u)
            sp.wait_ge(S("mix_lo"), NT)
            for u in (4, 5):
                load_unit(sp, 0, u)

            def load_expert(e):
                for u in range(6):
                    wait_lo(sp, e - 1, u)
                    load_unit(sp, e, u)
            load_expert(1)
            sp.wait_ge(S("counts_ready"), 3)
            sp.wait_ge(S("x1_stored"), 16 * NT)
            _first, last = first_last(sp, NE - 1)
            with sp.Fori(last + 1, YT) as t:
                sp.dma_start(y_dram[ds(t * P, P), :], x1_dram[0:P, :]).then_inc(S("rest_filled"), 16)
            with sp.Fori(2, NE) as e:
                load_expert(e)
            for u in range(6):
                wait_lo(sp, NE - 1, u)
            for i in range(NT):
                M = rows_of(i)
                sp.dma_start(x1c[i][0:M], x1_dram[i * P:i * P + M, :]).then_inc(S(f"x1_back{i}"), 16)
            sp.dma_start(bc_g2, ln2_g[0:1, :].to_broadcast((P, D))).then_inc(S("ln2_rows"), 16)
            sp.dma_start(bc_b2, ln2_b[0:1, :].to_broadcast((P, D))).then_inc(S("ln2_rows"), 16)
            for i in range(NT):
                sp.wait_ge(S("out_ready"), i + 1)
                sp.dma_start(ys if i == NT - 1 else yp[i * P:(i + 1) * P, :], x1c[i][0:rows_of(i)]
                             ).then_inc(S("stored"), 16)
            sp.wait_ge(S("stored"), 16 * NT)

        @block.gpsimd
        def _(pool):
            own = Tally(S("pool_setup"))

            def then(ins):
                pool.wait_ge(own.sem, own(ins))
            own(pool.memset(ident, 0.0))
            own(pool.memset(ones, 1.0))
            own(pool.memset(TRI[:, :, :], 1.0))
            own(pool.memset(wpool, 0.0))
            own(pool.memset(epsc, EPS))
            for a, hist in ((aP, HA), (bP, HB), (cP, HC)):
                own(pool.memset(a[:, :, 0:hist], 0.0))
            own(pool.iota(tpos, [[1, HB + 1]], base=1, channel_multiplier=0, allow_small_or_imprecise_dtypes=True))
            pool.wait_ge(own.sem, own.n)
            pool.affine_select(out=ident, in_=ident, compare_op=ALU.not_equal, fill=1.0, base=0,
                               pattern=[[-1, P]], channel_multiplier=1).then_inc(S("ident_ready"), 1)
            pool.affine_select(out=TRI[:, 0, :], in_=TRI[:, 0, :], compare_op=ALU.is_gt, fill=0.0, base=0,
                               pattern=[[1, P]], channel_multiplier=-1).then_inc(S("ident_ready"), 1)
            def win_lo(n, q):
                pool.wait_ge(S("win_hi"), n + 1)
                pool.tensor_tensor(win[:, q, 1], wraw[q].rearrange("p (k m) -> p k m", k=KD),
                                   win[:, q, 0].bitcast(F32), ALU.subtract).then_inc(S("win_lo"), 1)

            def gate_mul(m, n, P_, S_, c, hist):
                pool.wait_ge(S("projected"), n)
                pool.wait_ge(S("history_in"), 4)
                p_, s_ = P_[:, ds(c, 1), hist:hist + SEQ], S_[:, ds(c, 1), :, hist:hist + DECT]
                pool.tensor_tensor(p_, p_, gs[:, 0:SEQ].rearrange("p (a t) -> p a t", a=1), ALU.mult
                                   ).then_inc(S("gate_mul"), 1)
                pool.tensor_tensor(s_, s_, gs[:, SEQ:].rearrange("p (a b t) -> p a b t", a=1, b=DECB), ALU.mult
                                   ).then_inc(S("gate_mul"), 1)

            win_lo(0, 0)
            win_lo(1, 1)
            for g in range(4):
                h = 64 * (g % 2)
                pool.dma_start(wpool[h:h + 64, (g // 2) * P + h:(g // 2) * P + h + 64], w_pool[0, g]
                               ).then_inc(S("wpool_in"), 16)
            pool.dma_start(wrt.rearrange("p (k c) -> p k c", k=KD)[:, :, 0:NG],
                           w_rg[0].rearrange("(k p) c -> p k c", p=P)).then_inc(S("router_in"), 16)
            pool.dma_start(wrt.rearrange("p (k c) -> p k c", k=KD)[:, :, NG:NG + NE],
                           w_re[0].rearrange("(k p) c -> p k c", p=P)).then_inc(S("router_in"), 16)
            pool.dma_start(brt[:, 0:NG], b_rg[0:1, :].to_broadcast((P, NG))).then_inc(S("router_in"), 16)
            pool.dma_start(brt[:, NG:], b_re[0:1, :].to_broadcast((P, NE))).then_inc(S("router_in"), 16)
            with pool.Fori(0, CA) as c:
                win_lo(2 * c + 2, 0)
                gate_mul(c, 2 * c + 2, aP, aS, c, HA)
                win_lo(2 * c + 3, 1)

            sums = Tally(S("window_sums"))
            t, u = wsum_p, wsum_s

            def window_sum(c, i):
                lo, step = 2 ** (i + 1) - 1, 2 ** i
                a = bP[:, c] if i == 0 else t[(i - 1) % 2]
                b = bS[:, c] if i == 0 else u[(i - 1) % 2]
                if i > 0:
                    pool.wait_ge(sums.sem, sums.n)
                sums(pool.tensor_tensor(t[i % 2][:, lo:LB], a[:, lo:LB], a[:, lo - step:LB - step], ALU.add))
                sums(pool.tensor_tensor(u[i % 2][:, :, lo:LBS], b[:, :, lo:LBS], b[:, :, lo - step:LBS - step],
                                        ALU.add))

            def minus_token(c):
                pool.wait_ge(sums.sem, sums.n)
                m = mix[:, CA + c]
                for h in range(2):
                    r = slice(64 * h, 64 * h + 64)
                    if c + h > 0:
                        pool.wait_ge(S("pool_head"), 2 * c + h)
                    pool.tensor_tensor(m[r, 0:HB + 1], t[h][r, HB:2 * HB + 1], rc[r, c], ALU.mult
                                       ).then_inc(S("pool_head"), 1)
                pool.wait_ge(S("pool_head"), 2 * (c + 1))
                pool.wait_ge(S("window_scaled"), c + 1)
                pool.tensor_tensor(m[:, 0:SEQ], m[:, 0:SEQ], bP[:, c, HB:], ALU.subtract).then_inc(S("pooled"), 1)
                ms = m[:, SEQ:].rearrange("p (b t) -> p b t", b=DECB)
                pool.tensor_tensor(ms, ms, bS[:, c, :, HB:], ALU.subtract).then_inc(S("pooled"), 1)

            def short_conv(c):
                o, p1, p2 = prods[c]
                pool.wait_ge(S("tap_products"), c + 1)
                pool.tensor_tensor(o, o, p1, ALU.add).then_inc(S("short_conv"), 1)
                pool.wait_ge(S("short_conv"), 2 * c + 1)
                pool.tensor_tensor(o, o, p2, ALU.add).then_inc(S("short_conv"), 1)

            win_lo(N_U + 2, 0)
            pool.wait_ge(S("projected"), N_U + 1)
            for i in range(2):
                window_sum(0, i)
            win_lo(N_U + 3, 1)
            pool.wait_ge(S("rcnt_ready"), 1)
            minus_token(0)
            pool.wait_ge(S("projected"), N_U + 2)
            window_sum(1, 0)
            win_lo(N_C + 2, 0)
            window_sum(1, 1)
            window_sum(1, 2)
            win_lo(N_C + 3, 1)
            gate_mul(3, N_C + 2, cP, cS, 0, HC)
            window_sum(1, 3)
            win_lo(N_C + 4, 0)
            win_lo(N_C + 5, 1)
            gate_mul(4, N_C + 4, cP, cS, 1, HC)
            minus_token(1)
            win_lo(N_BG, 0)
            short_conv(0)
            win_lo(N_BG + 1, 1)
            gate_mul(5, N_C + 6, cP, cS, 2, HC)
            short_conv(1)
            win_lo(NCH - 1, 0)
            short_conv(2)

            wo_lo(pool, 0)
            pool.wait_ge(S("mix_lo"), 1)
            mix_lo(pool, 1)
            pool.wait_ge(S("ln1_rows"), 48)
            own2 = Tally(S("route_consts"))
            for i in range(NT - 1):
                M = rows_of(i)
                r = trow[(i + 2) % 3][0:M]
                if i + 2 < NT:
                    mix_lo(pool, i + 2)
                else:
                    pool.wait_ge(S("mix_lo"), NT)
                    for dst, n, base, step, mult in ((ig, P, 0, 1, 0), (it, NTAB, 0, 1, 0), (tokid[:, 0:NT], NT, 0, P, 0),
                                                     (tokid[:, NT:], 1, 0, 0, 1), (dsc, EPG, EPG, -1, 0)):
                        own2(pool.iota(dst, [[step, n]], base=base, channel_multiplier=mult,
                                       allow_small_or_imprecise_dtypes=True))
                pool.wait_ge(S("x1_normed"), i + 1)
                pool.tensor_tensor(r, r, bc_g1[0:M], ALU.mult).then_inc(S("x1_scaled"), 1)
                pool.wait_ge(S("x1_scaled"), i + 1)
                pool.tensor_tensor(r, r, bc_b1[0:M], ALU.add).then_inc(S("x1_ready"), 1)

            pool.memset(carrier[:, 0:1], 0.0).then_inc(S("y_free"), 1)
            pool.memset(carrier[:, 1:2], 0.0).then_inc(S("y_copied"), 1)

            def gather(t):
                pool.tensor_copy(idxc, table[:, ds(t, 1)]).then_inc(S("index_copied"), 1)
                pool.wait_ge(S("index_copied"), t + 1)
                pool.tensor_tensor(carrier[:, 0:1], epsc, epsc, ALU.add)
                pool.indirect_dma_start(xg, None, x1_dram, bass.IndirectOffsetOnAxis(ap=idxc, axis=0)
                                        ).then_inc(S("rows_in"), 16)

            for u in (0, 2, 3, 4):
                lo_unit(pool, 0, u)
            pool.wait_ge(S("table_ready"), 1)
            pool.wait_ge(S("x1_stored"), 16 * NT)
            gather(0)
            pool.wait_ge(S("unit_lo_rest"), 1)
            lo_unit(pool, 0, 5)
            pool.wait_ge(S("xe_turned"), 1)
            gather(1)

            def tile(t, e, last):
                if last:
                    lo_unit(pool, e + 1, LO_REST[0])
                pool.wait_ge(S("xe_turned"), t + 2)
                gather(t + 2)
                pool.wait_ge(S("y_copied"), t + 2)
                pool.dma_start(y_dram[ds(t * P, P), :], yrow).then_inc(S("y_stored"), 16)
                if last:
                    lo_unit(pool, e + 1, LO_REST[1])
                pool.wait_ge(S("y_stored"), 16 * t + 16)
                pool.tensor_tensor(carrier[:, 1:2], epsc, epsc, ALU.add).then_inc(S("y_free"), 1)
            pool.wait_ge(S("counts_ready"), 3)
            _first, last = first_last(pool, NE - 1)
            rest = pool.value_load(NTI[0:1, 2 * NE:], min_val=1, max_val=YT)
            expert_tiles(pool, tile)

            pool.wait_ge(S("rest_filled"), 16 * rest)
            pool.wait_ge(S("y_stored"), 16 * last + 16)
            pool.wait_ge(S("rows_in"), 16 * last + 48)
            pool.tensor_tensor(carrier[:, 2:3], epsc, epsc, ALU.add)

            def gather_y(i):
                M = rows_of(i)
                if i >= 4 + DVE_WEIGHS:
                    pool.wait_ge(S("y_summed"), i - 4 - DVE_WEIGHS + 1)
                elif i >= 4:
                    pool.wait_ge(S("out_weighed"), i - 4 + 1)
                for c in range(2):
                    pool.indirect_dma_start(yg[2 * (i % 4) + c][0:M], None, y_dram,
                                            bass.IndirectOffsetOnAxis(ap=slot[0:M, c, i:i + 1], axis=0)
                                            ).then_inc(S(f"y_back{i % 4}"), 16)
            for i in range(4):
                gather_y(i)
            pool.wait_ge(S("ln2_rows"), 32)
            for i in range(NT - 1):
                M = rows_of(i)
                for n in (4, 5) if i == 0 else (i + 5,):
                    if n < NT:
                        gather_y(n)
                if i in POOL_SCALES:
                    pool.wait_ge(S("out_normed"), i + 1)
                    pool.tensor_tensor(x1c[i][0:M], x1c[i][0:M], bc_g2[0:M], ALU.mult).then_inc(S("out_scaled_pool"), 1)
                    pool.wait_ge(S("out_scaled_pool"), POOL_SCALES.index(i) + 1)
                else:
                    pool.wait_ge(S("out_scaled"), DVE_SCALES.index(i) + 1)
                pool.tensor_tensor(x1c[i][0:M], x1c[i][0:M], bc_b2[0:M], ALU.add).then_inc(S("out_ready"), 1)

        @block.scalar
        def _(act):
            def win_hi(n, q):
                act.wait_ge(S(f"win_raw{q}"), 16 * ((n - q) // 2 + 1) if isinstance(n, int) else (n - q) * 8 + 16)
                act.activation(win[:, q, 0], wraw[q].rearrange("p (k m) -> p k m", k=KD), ACT.Copy
                               ).then_inc(S("win_hi"), 1)
            win_hi(0, 0)

            def x_hi(i, q, M):
                act.wait_ge(S("x_turned"), i + 1)
                for h in range(2):
                    act.activation(xT[:, 0, 4 * h:4 * h + 4, ds(i * P, M)],
                                   bank(2 * q + h).rearrange("p (k m) -> p k m", k=4)[:, :, 0:M], ACT.Copy
                                   ).then_inc(S("x_hi"), 1)
            with act.Fori(0, 2) as i:
                for q in range(4):
                    x_hi(4 * i + q, q, P)
            x_hi(NT - 1, 0, NS)
            win_hi(1, 1)

            def evacuate(n, q, col_, func, dst_p, dst_s):
                act.wait_ge(S("multiplied"), n + 1)
                b = pcol(col_)
                for g in range(2):
                    act.activation(dst_p(g * GRP, GRP), bank(3 * q + g, GRP), func, bias=b)
                act.activation(dst_p(2 * GRP, LASTP), bank(3 * q + 2, LASTP), func, bias=b)
                act.activation(dst_s, bank(3 * q + 2, GRP)[:, LASTP:].rearrange("p (b t) -> p b t", b=DECB),
                               func, bias=b).then_inc(S("projected"), 1)

            def to_ext(n, q, col_, P_, S_, c, hist, func=ACT.Identity):
                evacuate(n, q, col_, func,
                         lambda a, m: P_[:, ds(c, 1), hist + a:hist + a + m].rearrange("p a t -> p (a t)"),
                         S_[:, ds(c, 1), :, hist:hist + DECT].rearrange("p a b t -> p (a b) t"))

            def to_gs(n, q, col_, func):
                evacuate(n, q, col_, func, lambda a, m: gs[:, a:a + m],
                         gs[:, SEQ:].rearrange("p (b t) -> p b t", b=DECB))

            act.wait_ge(S("vectors_ready"), 2)
            def gated(c):
                to_ext(2 * c, 0, BLK_VAL + c, aP, aS, c, HA)
                win_hi(2 * c + 2, 0)
                if not (isinstance(c, int) and c == 0):
                    act.wait_ge(S("gate_mul"), 2 * c)
                to_gs(2 * c + 1, 1, BLK_GATE + c, ACT.Sigmoid)
                win_hi(2 * c + 3, 1)
            gated(0)
            with act.Fori(1, CA) as c:
                gated(c)
            for q in range(CB):
                to_ext(N_U + q, q, BLK_U + q, bP, bS, q, HB)
                win_hi(N_U + q + 2, q)

            def window_scale(c):
                act.wait_ge(S("window_sums"), 4 if c == 0 else 12)
                m = mix[:, CA + c]
                for h in range(2):
                    r = slice(64 * h, 64 * h + 64)
                    w = winv[r, c:c + 1]
                    act.activation(m[r, HB + 1:SEQ], wsum_p[h][r, 2 * HB + 1:LB], ACT.Copy, scale=w)
                    mm = act.activation(m[r, SEQ:].rearrange("p (b t) -> p b t", b=DECB), wsum_s[h][r, :, HB:],
                                        ACT.Copy, scale=w)
                mm.then_inc(S("window_scaled"), 1)

            def tap_products(c):
                act.wait_ge(S("gate_mul"), 2 * (CA + c + 1))
                if c > 0:
                    act.wait_ge(S("short_conv"), 2 * c)
                for j in range(3):
                    w = pcol(COL_CW + j * CC + c)
                    act.activation(prods[c][j][:, 0:SEQ], cP[:, c, j:j + SEQ], ACT.Copy, scale=w)
                    mm = act.activation(prods[c][j][:, SEQ:].rearrange("p (b t) -> p b t", b=DECB),
                                        cS[:, c, :, j:j + DECT], ACT.Copy, scale=w)
                mm.then_inc(S("tap_products"), 1)
            act.wait_ge(S("rcnt_ready"), 1)
            window_scale(0)
            for c in range(CC):
                to_ext(N_C + 2 * c, 0, BLK_CG + c, cP, cS, c, HC)
                win_hi(N_C + 2 * c + 2, 0)
                if c == 2:
                    act.wait_ge(S("pooled"), 4)
                    tap_products(0)
                act.wait_ge(S("gate_mul"), 2 * (CA + c))
                to_gs(N_C + 2 * c + 1, 1, BLK_H + c, ACT.Identity)
                win_hi(N_C + 2 * c + 3, 1)
                if c == 1:
                    window_scale(1)

            def state_out(name, dst, rows, n, sem):
                misc_ready(act, name)
                act.activation(dst[0:rows], bank(MB[name], n, rows), ACT.Copy).then_inc(S(sem), 1)
            for j in range(3):
                state_out(f"a{j}", out_a[:, j, :], min(PER_A, DECB - PER_A * j) * LAS, WA, "state_out_a")
            nb0 = min(PER_B, DECB)
            misc_ready(act, "b2")
            for name, h, dst, rows in (("b01", 0, out_b[:, 0, :], nb0 * LBS), ("b01", 1, out_b[:, 1, :], (DECB - nb0) * LBS),
                                       ("b2", 0, out_b[:, 2, :], HB)):
                act.activation(dst[0:rows], bank(MB[name], 512, rows)[:, h * WB:(h + 1) * WB], ACT.Copy
                               ).then_inc(S("state_out_bc"), 1)
            state_out("a3", out_ap, HA, WA, "state_out_bc")
            for c in range(CB):
                for g in range(3):
                    misc_ready(act, f"p{c}{g}")
                    act.activation(mix[:, CA + c, g * GRP:(g + 1) * GRP], bank(MB[f"p{c}{g}"], GRP), ACT.Copy,
                                   scale=pcol(COL_PS + c)).then_inc(S("pool_out"), 1)
            tap_products(1)
            act.wait_ge(S("multiplied"), N_BG + 1)
            win_hi(NCH - 1, 0)

            def square(g):
                act.wait_ge(S("centred"), 3 * (g + 1))
                if g > 0:
                    misc_ready(act, f"v{g - 1}")
                act.activation(squares, mix[:, 0:CA, g * GRP:(g + 1) * GRP], ACT.Square).then_inc(S("squared"), 1)
            act.wait_ge(S("win_lo"), NCH - 1)
            square(0)
            state_out("c0", out_c, DECB * LCS, WC, "state_out_bc")
            state_out("c1", out_cp, HC, WC, "state_out_bc")
            def deviation(g):
                misc_ready(act, f"v{g}")
                act.activation(stdev[g], bank(MB[f"v{g}"], GRP), ACT.Sqrt, bias=epsc, scale=1.0 / WA
                               ).then_inc(S("stdev_a"), 1)
            square(1)
            act.wait_ge(S("win_lo"), NCH)
            deviation(0)
            square(2)
            deviation(1)
            tap_products(2)
            deviation(2)

            def swish(g):
                for c in range(CA):
                    act.wait_ge(S("ln_a_norm"), 3 * g + c + 1)
                    m = mix[:, c, g * GRP:(g + 1) * GRP]
                    act.activation(m, m, ACT.Silu, bias=pcol(COL_B + c), scale=pcol(COL_G + c)
                                   ).then_inc(S("swished"), 1)

            def wo_hi(u):
                act.wait_ge(S("xT_used" if u < 3 else "multiplied"), u + 1 if u < 3 else NCH)
                act.wait_ge(S(f"wo_raw{u}"), 16)
                act.activation(unit_parts(u)[0], unit_raw(u), ACT.Copy).then_inc(S("wo_hi"), 1)

            def mix_hi(i):
                M = rows_of(i)
                act.activation(mhl[:, i % 2, 0, :, 0:M], mix[:, :, i * P:i * P + M], ACT.Copy).then_inc(S("mix_hi"), 1)
            swish(0)
            wo_hi(0)
            swish(1)
            wo_hi(1)
            swish(2)
            act.wait_ge(S("swished"), 3 * CA)
            act.wait_ge(S("pool_out"), 6)
            act.wait_ge(S("short_done"), 3 * CC)
            mix_hi(0)
            wo_hi(2)
            wo_hi(3)
            mix_hi(1)

            def turn_copy(i):
                M = rows_of(i)
                act.wait_ge(S("x1_turned"), i + 1)
                act.wait_ge(S("routed"), i)
                act.activation(x1T[:, :, 0:M], PS[:, 4:6, :].rearrange("p b (k m) -> p (b k) m", k=4)[:, :, 0:M],
                               ACT.Copy).then_inc(S("x1T_ready"), 1)
            def hi_unit(e, u):
                h, _l = unit_parts(u)
                act.wait_ge(S(f"unit_raw{u}"), (32 if u < 4 else 16) * (e + 1))
                act.activation(h, unit_raw(u), ACT.Copy).then_inc(S("unit_hi"), 1)
            for i in range(NT):
                M = rows_of(i)
                if i + 2 < NT:
                    act.wait_ge(S("out_multiplied"), i + 1)
                    mix_hi(i + 2)
                if i == NT - 1:
                    act.wait_ge(S("out_multiplied"), NT)
                    hi_unit(0, 0)
                act.wait_ge(S("stats1"), i + 1)
                act.activation(sd[i % 2][0:M], mv[i % 2][0:M, 1:2], ACT.Sqrt, bias=epsc[0:M]).then_inc(S("stdev1"), 1)
                if i == NT - 1:
                    turn_copy(i - 1)
                act.wait_ge(S("norm1"), 2 * (i + 1))
                r = trow[(i + 2) % 3][0:M]
                act.activation(r, r, ACT.Identity, bias=nmr[i % 2][0:M], scale=rstd[i % 2][0:M]
                               ).then_inc(S("x1_normed"), 1)
                if 0 < i < NT - 1:
                    turn_copy(i - 1)

            for u in (1, 2):
                hi_unit(0, u)
            turn_copy(NT - 1)
            hi_unit(0, 3)
            act.wait_ge(S("logits_less"), 1)
            act.activation(g36[4], g36[3], ACT.Exp).then_inc(S("exps"), 1)
            act.wait_ge(S("logits_less"), 2)
            act.activation(g9[5], g9[4], ACT.Exp).then_inc(S("exps"), 1)
            for u in (4, 5):
                hi_unit(0, u)

            def xe_hi(t):
                act.wait_ge(S("xe_turned"), t + 1)
                act.activation(xe[:, 0], PS[:, 2:4, :].rearrange("p b (k m) -> p (b k) m", k=4), ACT.Copy
                               ).then_inc(S("xe_hi"), 1)
            for h, sem in enumerate(("half_turned", "xe_turned")):
                act.wait_ge(S(sem), 1)
                act.activation(xe[:, 0, 4 * h:4 * h + 4], bank(2 + h).rearrange("p (k m) -> p k m", k=4), ACT.Copy
                               ).then_inc(S("half_hi" if h == 0 else "xe_hi"), 1)

            def tile(t, e, last):
                act.wait_ge(S("first_half"), t + 1)
                act.activation(hid[:, 0:256], bank(0)[:, 0:256], ACT.Silu).then_inc(S("silu_done"), 1)
                act.wait_ge(S("hid_turned"), 2 * t + 1)
                act.activation(he[:, 0, 0:2, :], bank(4)[:, 0:256].rearrange("p (k m) -> p k m", k=2), ACT.Copy
                               ).then_inc(S("he_hi"), 1)
                if last:
                    for u in (0, 1):
                        act.wait_ge(S("unit_used"), 6 * t + u + 1)
                        hi_unit(e + 1, u)
                act.wait_ge(S("unit_used"), 6 * t + 4)
                act.activation(hid[:, 256:512], bank(1)[:, 0:256], ACT.Silu).then_inc(S("silu_done"), 1)
                xe_hi(t + 1)
                act.wait_ge(S("hid_turned"), 2 * t + 2)
                act.activation(he[:, 0, 2:4, :], bank(4)[:, 256:512].rearrange("p (k m) -> p k m", k=2), ACT.Copy
                               ).then_inc(S("he_hi"), 1)
                if last:
                    for u in (2, 3):
                        hi_unit(e + 1, u)
                act.wait_ge(S("unit_used"), 6 * t + 6)
                act.wait_ge(S("y_free"), t + 1)
                act.activation(yrow, PS[:, 5:7, :].rearrange("p b n -> p (b n)"), ACT.Copy).then_inc(S("y_copied"), 1)
                if last:
                    for u in (4, 5):
                        hi_unit(e + 1, u)
            expert_tiles(act, tile)

            def diagonals(i):
                for c in range(2):
                    act.activation(diag[:, i % 2, c], ident, ACT.Copy, scale=wgt[:, c, i:i + 1]
                                   ).then_inc(S("diag_made"), 1)
            diagonals(DVE_WEIGHS)
            diagonals(DVE_WEIGHS + 1)
            for i in range(NT):
                M = rows_of(i)
                act.wait_ge(S(f"x1_back{i}"), 16)
                act.activation(x1c[i][0:M], x1c[i][0:M], ACT.Copy, scale=ALPHA).then_inc(S("x1_alpha"), 1)
            for i in range(NT):
                M = rows_of(i)
                if DVE_WEIGHS <= i < NT - 2:
                    act.wait_ge(S("y_summed"), i - DVE_WEIGHS + 1)
                    diagonals(i + 2)
                act.wait_ge(S("stats2"), i + 1)
                act.activation(sd[i % 2][0:M], mv[i % 2][0:M, 1:2], ACT.Sqrt, bias=epsc[0:M]).then_inc(S("stdev2"), 1)
                act.wait_ge(S("norm2"), 2 * (i + 1))
                act.activation(x1c[i][0:M], x1c[i][0:M], ACT.Identity, bias=nmr[i % 2][0:M], scale=rstd[i % 2][0:M]
                               ).then_inc(S("out_normed"), 1)

        @block.vector
        def _(dve):
            own = Tally(S("dve_setup"))
            for c in range(CB):
                for h in range(2):
                    w = 2.0 ** (2 * c + h + 1)
                    own(dve.memset(winv[64 * h:64 * h + 64, c:c + 1], 1.0 / w))
                    own(dve.memset(wmin[64 * h:64 * h + 64, c:c + 1], w))
            dve.wait_ge(own.sem, own.n)
            dve.wait_ge(S("ident_ready"), 2)
            for c in range(CB):
                own(dve.tensor_scalar(rc[:, c], tpos, wmin[:, c:c + 1], None, ALU.min))
            dve.wait_ge(own.sem, own.n)
            dve.reciprocal(rcnt, rcnt).then_inc(S("rcnt_ready"), 1)

            def x_lo(i, q, M):
                for h in range(2):
                    dve.wait_ge(S("x_hi"), 2 * i + h + 1)
                    dve.tensor_tensor(xT[:, 1, 4 * h:4 * h + 4, ds(i * P, M)],
                                      bank(2 * q + h).rearrange("p (k m) -> p k m", k=4)[:, :, 0:M],
                                      xT[:, 0, 4 * h:4 * h + 4, ds(i * P, M)].bitcast(F32), ALU.subtract
                                      ).then_inc(S("x_lo"), 1)
            with dve.Fori(0, 2) as i:
                for q in range(4):
                    x_lo(4 * i + q, q, P)
            x_lo(NT - 1, 0, NS)
            dve.wait_ge(S("small_turned"), 2)
            dve.tensor_copy(pcA, bank(4, TAPS * CA)).then_inc(S("vectors_ready"), 1)
            dve.tensor_copy(pcB, bank(4)[:, P:P + 37]).then_inc(S("vectors_ready"), 1)
            dve.wait_ge(S("small_turned"), 6)
            for h in range(2):
                dve.tensor_copy(aS[:, :, 4 * h:4 * h + 4, 0:HA],
                                bank(5 + h, 360).rearrange("p (c b t) -> p c b t", c=CA, b=4)
                                ).then_inc(S("history_in"), 1)
            dve.tensor_copy(bS[:, :, :, 0:HB], bank(7, 240).rearrange("p (c b t) -> p c b t", c=CB, b=DECB)
                            ).then_inc(S("history_in"), 1)
            dve.tensor_copy(cS[:, :, :, 0:HC], bank(7)[:, 256:304].rearrange("p (c b t) -> p c b t", c=CC, b=DECB)
                            ).then_inc(S("history_in"), 1)

            def conv_a(c):
                dve.wait_ge(S("gate_mul"), 2 * (c + 1))
                taps(dve, c, TAPS, lambda j: pcA[:, ds(j * CA + c, 1)], pcol(COL_CB + c), aP, aS, mix,
                     S("conv_taps"), 3 * TAPS * c)

            with dve.Fori(0, CA) as c:
                conv_a(c)

            for g in range(3):
                misc_ready(dve, f"m{g}")
                for c in range(CA):
                    m = mix[:, c, g * GRP:(g + 1) * GRP]
                    dve.scalar_tensor_tensor(m, bank(MB[f"m{g}"], GRP), -1.0 / WA, m, ALU.mult, ALU.add
                                             ).then_inc(S("centred"), 1)

            def norm_a(g):
                dve.wait_ge(S("stdev_a"), g + 1)
                dve.reciprocal(stdev[g], stdev[g]).then_inc(S("rstd_a"), 1)
                dve.wait_ge(S("rstd_a"), g + 1)
                for c in range(CA):
                    m = mix[:, c, g * GRP:(g + 1) * GRP]
                    dve.tensor_tensor(m, m, stdev[g], ALU.mult).then_inc(S("ln_a_norm"), 1)

            def short_mul(c):
                dve.wait_ge(S("multiplied"), N_BG + c + 1)
                dve.wait_ge(S("short_conv"), 2 * (c + 1))
                for g in range(3):
                    m = mix[:, 5 + c, g * GRP:(g + 1) * GRP]
                    dve.scalar_tensor_tensor(m, bank(3 * (c % 2) + g, GRP), pcol(BLK_BG + c), m, ALU.add, ALU.mult
                                             ).then_inc(S("short_done"), 1)
            short_mul(0)
            short_mul(1)
            for g in range(3):
                norm_a(g)
            short_mul(2)

            mix_lo(dve, 0)
            dve.wait_ge(S("wo_lo"), 1)
            for u in range(1, 4):
                wo_lo(dve, u)
            dve.wait_ge(S("pool_out"), 6)
            dve.memset(L[:, NT - 1, :], 0.0).then_inc(S("logits_cleared"), 1)
            dve.wait_ge(S("ln1_rows"), 48)

            def stats(i, r, sem):
                q, M = i % 2, rows_of(i)
                for h in range(2):
                    dve.bn_stats(bn[q][0:M, h], r[:, h * 512:(h + 1) * 512]).then_inc(S("bn_steps" + sem), 1)
                dve.wait_ge(S("bn_steps" + sem), 2 * (i + 1))
                dve.bn_aggr(mv[q][0:M], bn[q][0:M].rearrange("p h s -> p (h s)")).then_inc(S("stats" + sem), 1)

            def scales(i, sem):
                q, M = i % 2, rows_of(i)
                dve.wait_ge(S("stdev" + sem), i + 1)
                dve.reciprocal(rstd[q][0:M], sd[q][0:M]).then_inc(S("norm" + sem), 1)
                dve.wait_ge(S("norm" + sem), 2 * i + 1)
                dve.scalar_tensor_tensor(nmr[q][0:M], mv[q][0:M, 0:1], -1.0, rstd[q][0:M], ALU.mult, ALU.mult
                                         ).then_inc(S("norm" + sem), 1)

            def logits(i):
                M = rows_of(i)
                dve.wait_ge(S("routed"), i + 1)
                dve.tensor_tensor(L[0:M, i, :], bank(6, NG + NE, M), brt[0:M], ALU.add).then_inc(S("logits"), 1)

            for i in range(NT):
                M = rows_of(i)
                r = trow[(i + 2) % 3][0:M]
                dve.wait_ge(S(f"x_again{i % 3}"), 16 * (i // 3 + 1))
                dve.scalar_tensor_tensor(r, r, ALPHA, bc_bo[0:M], ALU.mult, ALU.add).then_inc(S("residual"), 1)
                dve.wait_ge(S("residual"), i + 1)
                dve.wait_ge(S("out_multiplied"), i + 1)
                for h in range(2):
                    dve.tensor_tensor(r[:, h * 512:(h + 1) * 512], bank(2 * (i % 2) + h, rows=M),
                                      r[:, h * 512:(h + 1) * 512], ALU.add).then_inc(S("out_taken"), 1)
                dve.wait_ge(S("out_taken"), 2 * (i + 1))
                if i >= 2:
                    dve.wait_ge(S("x1_normed"), i - 1)
                stats(i, r, "1")
                scales(i, "1")
                if i > 1:
                    logits(i - 2)
            dve.wait_ge(S("x1_normed"), NT)
            dve.wait_ge(S("x1_scaled"), NT - 1)
            dve.tensor_tensor(r, r, bc_g1[0:M], ALU.mult).then_inc(S("x1_scaled"), 1)
            logits(NT - 2)
            dve.wait_ge(S("x1_scaled"), NT)
            dve.wait_ge(S("x1_ready"), NT - 1)
            dve.tensor_tensor(r, r, bc_b1[0:M], ALU.add).then_inc(S("x1_ready"), 1)
            lo_unit(dve, 0, 1)
            logits(NT - 1)

            step = Tally(S("route_steps"))

            def do(ins):
                dve.wait_ge(step.sem, step(ins))

            def over(a, n):
                return a.rearrange("p (i o) -> p i o", o=1).to_broadcast((P, NT, n))

            def last4(a):
                return a.rearrange("p (o c) -> p o c", o=1).to_broadcast((P, NT, NG))
            dve.wait_ge(S("logits"), NT)
            dve.wait_ge(S("logits_cleared"), 1)
            dve.wait_ge(S("route_consts"), 5)
            G, E = L[:, :, 0:NG], L[:, :, NG:]

            def first_max(v, top, eq, ohv, m):
                do(dve.tensor_reduce(top, v, AX, ALU.max))
                do(dve.tensor_tensor(eq, v, over(top, NG), ALU.is_equal))
                do(dve.tensor_tensor(eq, eq, last4(dsc), ALU.mult))
                do(dve.tensor_reduce(m, eq, AX, ALU.max))
                do(dve.tensor_tensor(ohv, last4(dsc), over(m, NG), ALU.is_equal))
            gmax, gsum, gp, v1, dv, ex, v2, m9, w1, rs = g9
            eq, ohg, oh1, gd, ge, esel, oh2, esel2 = g36
            first_max(G, gmax, eq, ohg, m9)
            dve.tensor_tensor(gd, G, over(gmax, NG), ALU.subtract).then_inc(S("logits_less"), 1)
            do(dve.tensor_tensor(prod, E.rearrange("p i (g j) -> p i g j", g=NG),
                                 ohg.rearrange("p i (g o) -> p i g o", o=1).to_broadcast((P, NT, NG, EPG)), ALU.mult))
            do(dve.tensor_reduce(esel, prod.rearrange("p i g j -> p i j g"), AX, ALU.add))
            first_max(esel, v1, eq, oh1, m9)
            do(dve.scalar_tensor_tensor(esel2, oh1, -3.0e38, esel, ALU.mult, ALU.add))
            first_max(esel2, v2, eq, oh2, m9)
            dve.tensor_tensor(dv, v2, v1, ALU.subtract).then_inc(S("logits_less"), 1)
            for OH, oh in ((OH1, oh1), (OH2, oh2)):
                do(dve.tensor_tensor(OH, ohg.rearrange("p i (g o) -> p i g o", o=1).to_broadcast((P, NT, NG, EPG)),
                                     oh.rearrange("p i (o j) -> p i o j", o=1).to_broadcast((P, NT, NG, EPG)), ALU.mult))
            flat = [o.rearrange("p i g j -> p i (g j)") for o in (OH1, OH2)]
            do(dve.tensor_tensor(Mb, flat[0], flat[1], ALU.add))
            for lo in range(NS, P, 32):
                dve.memset(Mb[lo:lo + 32, NT - 1, :], 0.0).then_inc(S("choices"), 1)
            dve.wait_ge(S("ranked"), 1)
            counts_ps = bank(7)[:, NT * NE:(NT + 1) * NE]
            ciI, ci2I = ci.bitcast(I32), ci2.bitcast(I32)
            do(dve.tensor_scalar(ciI, counts_ps, float(P - 1), None, ALU.add))
            do(dve.tensor_scalar(ci2I, ciI, 7, None, ALU.logical_shift_right))
            do(dve.tensor_scalar(ntf, ci2I, 1.0, None, ALU.max))
            do(dve.tensor_tensor_scan(inc, ones[:, 0:NE], ntf, 0.0, ALU.mult, ALU.add))
            do(dve.tensor_tensor(exc, inc, ntf, ALU.subtract))
            dve.tensor_copy(NTI[:, 0:NE], exc).then_inc(S("counts_ready"), 1)
            dve.tensor_scalar(NTI[:, NE:2 * NE], inc, -1.0, None, ALU.add).then_inc(S("counts_ready"), 1)
            dve.tensor_scalar(NTI[:, 2 * NE:], inc[:, NE - 1:], -1.0, float(YT), ALU.mult, ALU.add
                              ).then_inc(S("counts_ready"), 1)
            ri, rhi, rlo, rlf, tcol, slf = r18
            rk = bank(7, NT * NE).rearrange("p (i e) -> p i e", i=NT)
            key = prod.rearrange("p i g j -> p i (g j)")
            do(dve.scalar_tensor_tensor(key, exc.rearrange("p (o e) -> p o e", o=1).to_broadcast((P, NT, NE)), float(P),
                                        rk, ALU.mult, ALU.add))
            do(dve.tensor_tensor(OHB, OHB, key.rearrange("p (k i) e -> p k i e", k=1).to_broadcast((P, 2, NT, NE)),
                                 ALU.mult))
            do(dve.tensor_reduce(slf, OHB, AX, ALU.add))
            rI, rhI, rlI = ri.bitcast(I32), rhi.bitcast(I32), rlo.bitcast(I32)
            do(dve.tensor_copy(rI, slf))
            dve.tensor_copy(slot, slf).then_inc(S("slots_ready"), 1)
            do(dve.tensor_scalar(rhI, rI, 7, None, ALU.logical_shift_right))
            do(dve.tensor_copy(tcol, rhI))
            do(dve.tensor_scalar(rlI, rI, P - 1, None, ALU.bitwise_and))
            do(dve.tensor_copy(rlf, rlI))
            dve.wait_ge(S("x1_ready"), NT)
            four = (P, 2, NT, NTAB)
            do(dve.tensor_tensor(ohe, it.rearrange("p (k i m) -> p k i m", k=1, i=1).to_broadcast(four),
                                 tcol.rearrange("p k (i m) -> p k i m", m=1).to_broadcast(four), ALU.is_equal))
            do(dve.tensor_tensor(oht[:, :, :, 0, :], ohe, tokid[:, 0:NT].rearrange("p (k i m) -> p k i m", k=1, m=1
                                                                                   ).to_broadcast(four), ALU.mult))
            do(dve.tensor_scalar(oht[:, :, :, 1, :], ohe, tokid[:, NT:], None, ALU.mult))
            for c in range(2):
                dve.tensor_tensor(ohp[:, c], ig.rearrange("p (i m) -> p i m", i=1).to_broadcast((P, NT, P)),
                                  rlf[:, c].rearrange("p (i m) -> p i m", m=1).to_broadcast((P, NT, P)),
                                  ALU.is_equal).then_inc(S("one_hot"), 1)
            dve.wait_ge(S("exps"), 2)
            do(dve.tensor_reduce(gsum, ge, AX, ALU.add))
            do(dve.reciprocal(gp, gsum))
            do(dve.tensor_scalar(rs, ex, 1.0, None, ALU.add))
            do(dve.reciprocal(rs, rs))
            do(dve.tensor_tensor(wgt[:, 0], rs, gp, ALU.mult))
            do(dve.tensor_tensor(wgt[:, 1], wgt[:, 0], ex, ALU.mult))
            dve.wait_ge(S("table_sum"), 1)
            do(dve.tensor_copy(tabf, bank(6, 2 * NTAB)))
            dve.tensor_tensor(table, tabf[:, 0:NTAB], tabf[:, NTAB:], ALU.add).then_inc(S("table_ready"), 1)

            def xe_lo(t):
                dve.wait_ge(S("xe_hi"), t + 1)
                dve.tensor_tensor(xe[:, 1], PS[:, 2:4, :].rearrange("p b (k m) -> p (b k) m", k=4),
                                  xe[:, 0].bitcast(F32), ALU.subtract).then_inc(S("xe_lo"), 1)
            for h, sem in enumerate(("half_hi", "xe_hi")):
                dve.wait_ge(S(sem), 1)
                ins = dve.tensor_tensor(xe[:, 1, 4 * h:4 * h + 4], bank(2 + h).rearrange("p (k m) -> p k m", k=4),
                                        xe[:, 0, 4 * h:4 * h + 4].bitcast(F32), ALU.subtract)
            ins.then_inc(S("xe_lo"), 1)

            def tile(t, e, last):
                def hidden(h):
                    dve.wait_ge(S("silu_done"), 2 * t + h + 1)
                    v = hid[:, h * 256:(h + 1) * 256]
                    dve.tensor_tensor(v, v, bank(h)[:, 256:512], ALU.mult).then_inc(S("hidden"), 1)

                def he_lo(h):
                    dve.wait_ge(S("he_hi"), 2 * t + h + 1)
                    dve.tensor_tensor(he[:, 1, 2 * h:2 * h + 2, :],
                                      bank(4)[:, h * 256:(h + 1) * 256].rearrange("p (k m) -> p k m", k=2),
                                      he[:, 0, 2 * h:2 * h + 2, :].bitcast(F32), ALU.subtract).then_inc(S("he_lo"), 1)
                hidden(0)
                he_lo(0)
                if last:
                    lo_unit(dve, e + 1, 0)
                hidden(1)
                he_lo(1)
                xe_lo(t + 1)
                if last:
                    for u in (2, 3, 4):
                        lo_unit(dve, e + 1, u)
            expert_tiles(dve, tile)

            dve.memset(carrier[:, 3:4], 0.0).then_inc(S("tiles_left"), 1)
            dve.wait_ge(S("ln2_rows"), 32)

            def finish(i):
                M = rows_of(i)
                dve.wait_ge(S("out_normed"), i + 1)
                dve.tensor_tensor(x1c[i][0:M], x1c[i][0:M], bc_g2[0:M], ALU.mult).then_inc(S("out_scaled"), 1)
            for i in range(NT):
                M = rows_of(i)
                o = x1c[i][0:M]
                dve.wait_ge(S("x1_alpha"), i + 1)
                if i < DVE_WEIGHS:
                    dve.wait_ge(S(f"y_back{i}"), 32)
                    for c in range(2):
                        dve.scalar_tensor_tensor(o, yg[2 * i + c][0:M], wgt[0:M, c, i:i + 1], o, ALU.mult, ALU.add
                                                 ).then_inc(S("weigh_steps" if c == 0 else "out_weighed"), 1)
                        if c == 0:
                            dve.wait_ge(S("weigh_steps"), i + 1)
                else:
                    dve.wait_ge(S("y_summed"), i - DVE_WEIGHS + 1)
                    dve.tensor_tensor(o, o, PS[0:M, 2 * (i % 2):2 * (i % 2) + 2, :].rearrange("p b n -> p (b n)"),
                                      ALU.add).then_inc(S("out_weighed"), 1)
                dve.wait_ge(S("out_weighed"), i + 1)
                if i >= 2:
                    dve.wait_ge(S("out_normed"), i - 1)
                stats(i, o, "2")
                if i - 1 in DVE_SCALES:
                    finish(i - 1)
                scales(i, "2")
            finish(NT - 1)
            dve.wait_ge(S("out_scaled"), len(DVE_SCALES))
            dve.wait_ge(S("out_ready"), NT - 1)
            dve.tensor_tensor(x1c[NT - 1][0:NS], x1c[NT - 1][0:NS], bc_b2[0:NS], ALU.add).then_inc(S("out_ready"), 1)

        @block.tensor
        def _(pe):
            def turn(out, in_, n):
                return pe.transpose(out, in_, ident[0:n, 0:n])

            pe.wait_ge(S("ident_ready"), 2)
            for i in range(NT):
                M, q = rows_of(i), i % 4
                pe.wait_ge(S(f"x_rows{i}"), 16)
                if i >= 4:
                    pe.wait_ge(S("x_lo"), 2 * (i - 3))
                for c in range(KD):
                    mm = turn(bank(2 * q + c // 4)[:, (c % 4) * P:(c % 4) * P + M], xrow[i][0:M, c * P:(c + 1) * P], M)
                mm.then_inc(S("x_turned"), 1)

            def project(n, q, between=(), used=None):
                pe.wait_ge(S("win_lo"), n + 1)
                for c in range(KD):
                    for small in between[c - 1] if 0 < c <= len(between) else ():
                        small()
                    for ws, xs_ in ((0, 0), (0, 1), (1, 0)):
                        for g in range(3):
                            mm = pe.matmul(bank(3 * q + g, GRP), win[:, q, ws, c, :],
                                           xT[:, xs_, c, g * GRP:(g + 1) * GRP],
                                           start=(c == 0 and ws + xs_ == 0), stop=(c == KD - 1 and ws == 1))
                    if used and c in (1, 3, 5):
                        mm.then_inc(S(used), 1)
                mm.then_inc(S("multiplied"), 1)

            def turn_small():
                pe.wait_ge(S("vectors_in"), 16 * 7)
                turn(bank(4, TAPS * CA), vec_rows[0:TAPS * CA, 0, :], TAPS * CA).then_inc(S("small_turned"), 1)
                turn(bank(4)[:, P:P + 37], vec_rows[0:37, 1, :], 37).then_inc(S("small_turned"), 1)
                pe.wait_ge(S("states_in"), 16 * 4)
                for h in range(2):
                    for c in range(CA):
                        mm = turn(bank(5 + h)[:, c * 120:(c + 1) * 120], hist_a[0:120, h, c * P:(c + 1) * P], 120)
                    mm.then_inc(S("small_turned"), 1)
                for c in range(CB):
                    mm = turn(bank(7)[:, c * 120:(c + 1) * 120], hist_b[0:120, c * P:(c + 1) * P], 120)
                mm.then_inc(S("small_turned"), 1)
                for c in range(CC):
                    mm = turn(bank(7)[:, 256 + c * 16:256 + (c + 1) * 16], hist_c[0:16, c * P:(c + 1) * P], 16)
                mm.then_inc(S("small_turned"), 1)

            pe.wait_ge(S("x_lo"), 2 * NT)
            project(0, 0, ((), (), (), (), (turn_small,)))
            pe.wait_ge(S("vectors_ready"), 2)
            pe.wait_ge(S("history_in"), 4)
            project(1, 1)
            with pe.Fori(1, (N_BG) // 2) as i:
                for q in range(2):
                    pe.wait_ge(S("projected"), 2 * i + q - 1)
                    project(2 * i + q, q)

            def job(name):
                j = job_no[name]
                if j >= 2:
                    _n, s_, v = jobs[j - 2]
                    pe.wait_ge(S(s_), v)
                return bank(MB[name])

            def summed(name, src):
                o = job(name)
                for c in range(CA):
                    mm = pe.matmul(o[:, 0:GRP], ones, src(c), start=(c == 0), stop=(c == CA - 1))
                mm.then_inc(S("misc_done"), 1)

            def turn_rows(name, *srcs, chunks):
                o = job(name)
                for h, src in enumerate(srcs):
                    for c in range(chunks):
                        r = src(c)
                        mm = turn(o[0:r.shape[1], (h * chunks + c) * P:(h * chunks + c + 1) * P], r, P)
                mm.then_inc(S("misc_done"), 1)

            def sequences(S_, c, b0, n):
                return S_[:, c, b0:b0 + n, :].rearrange("p b t -> p (b t)")
            nb0 = min(PER_B, DECB)

            def state_a(j):
                return lambda: turn_rows(f"a{j}", lambda c: sequences(aS, c, PER_A * j, min(PER_A, DECB - PER_A * j)), chunks=CA)

            def state(name, chunks, *srcs):
                return lambda: turn_rows(name, *srcs, chunks=chunks)

            def pool_linear(c, g):
                return lambda: pe.matmul(job(f"p{c}{g}")[:, 0:GRP], wpool[:, c * P:(c + 1) * P],
                                         mix[:, CA + c, g * GRP:(g + 1) * GRP], start=True, stop=True
                                         ).then_inc(S("misc_done"), 1)

            def mean(g):
                def run():
                    pe.wait_ge(S("conv_taps"), 3 * TAPS * CA)
                    summed(f"m{g}", lambda c: mix[:, c, g * GRP:(g + 1) * GRP])
                return run

            def variance(g):
                def run():
                    pe.wait_ge(S("squared"), g + 1)
                    summed(f"v{g}", lambda c: squares[:, c])
                return run
            pe.wait_ge(S("gate_mul"), 2 * CA)
            pe.wait_ge(S("pooled"), 4)
            pe.wait_ge(S("wpool_in"), 64)
            pe.wait_ge(S("projected"), N_BG - 1)
            project(N_BG, 0, ((state_a(0), state_a(1)),
                              (state_a(2), state("b01", CB, lambda c: sequences(bS, c, 0, nb0),
                                                 lambda c: sequences(bS, c, nb0, DECB - nb0))),
                              (state("b2", CB, lambda c: bP[:, c, SEQ:]),),
                              (state("a3", CA, lambda c: aP[:, c, SEQ:]), pool_linear(0, 0)),
                              (pool_linear(0, 1), pool_linear(0, 2)), (pool_linear(1, 0), pool_linear(1, 1)),
                              (pool_linear(1, 2),)))
            pe.wait_ge(S("projected"), N_BG)
            pe.wait_ge(S("gate_mul"), 2 * (CA + CC))
            project(N_BG + 1, 1, ((mean(0),), (mean(1),), (mean(2),),
                                  (state("c0", CC, lambda c: sequences(cS, c, 0, DECB)),
                                   state("c1", CC, lambda c: cP[:, c, SEQ:])), (variance(0),), (), (variance(1),)))
            pe.wait_ge(S("short_done"), 3)
            project(N_BG + 2, 0, ((variance(2),),), "xT_used")

            def route(i):
                M = rows_of(i)
                pe.wait_ge(S("x1T_ready"), i + 1)
                pe.wait_ge(S("router_in"), 64)
                if i > 0:
                    pe.wait_ge(S("logits"), i)
                for c in range(KD):
                    mm = pe.matmul(bank(6, NG + NE, M), x1T[:, c, 0:M], wrt[:, c * 20:(c + 1) * 20],
                                   start=(c == 0), stop=(c == KD - 1))
                mm.then_inc(S("routed"), 1)

            def turn_x1(i):
                M = rows_of(i)
                pe.wait_ge(S("x1_ready"), i + 1)
                if i > 0:
                    pe.wait_ge(S("x1T_ready"), i)
                for c in range(KD):
                    mm = turn(bank(4 + c // 4)[:, (c % 4) * P:(c % 4) * P + M],
                              trow[(i + 2) % 3][0:M, c * P:(c + 1) * P], M)
                mm.then_inc(S("x1_turned"), 1)

            for i in range(NT):
                M = rows_of(i)
                pe.wait_ge(S("mix_lo"), i + 1)
                if i >= 2:
                    pe.wait_ge(S("out_taken"), 2 * (i - 1))
                for c in range(KD):
                    if i == 0 and c % 2 == 0:
                        pe.wait_ge(S("wo_lo"), c // 2 + 1)
                    for ms, ws in ((0, 0), (0, 1), (1, 0)):
                        for h in range(2):
                            mm = pe.matmul(bank(2 * (i % 2) + h, rows=M), mhl[:, i % 2, ms, c, 0:M],
                                           wo[:, ws, c, h * 512:(h + 1) * 512],
                                           start=(c == 0 and ms + ws == 0), stop=(c == KD - 1 and ms == 1))
                mm.then_inc(S("out_multiplied"), 1)
                if i > 1:
                    route(i - 2)
                if i > 0:
                    turn_x1(i - 1)
            route(NT - 2)
            turn_x1(NT - 1)
            route(NT - 1)

            pe.wait_ge(S("choices"), 3)
            rk = bank(7, NT * NE)
            mflat = Mb.rearrange("p i e -> p (i e)")
            pe.matmul(rk, TRI[:, 0, :], mflat, start=True, stop=False, skip_group_check=True)
            for i in range(NT - 1):
                n = NT - 1 - i
                pe.matmul(rk.rearrange("p (i e) -> p i e", i=NT)[:, i + 1:, :], TRI[:, 1, :],
                          Mb[:, i:i + 1, :].to_broadcast((P, n, NE)), start=False, stop=(i == NT - 2),
                          skip_group_check=True)
            for i in range(NT):
                mm = pe.matmul(bank(7)[:, NT * NE:(NT + 1) * NE], TRI[:, 1, :], Mb[:, i, :],
                               start=(i == 0), stop=(i == NT - 1), skip_group_check=True)
            mm.then_inc(S("ranked"), 1)
            for c in range(2):
                pe.wait_ge(S("one_hot"), c + 1)
                for i in range(NT):
                    M = rows_of(i)
                    mm = pe.matmul(bank(6, 2 * NTAB), ohp[0:M, c, i], oht[0:M, c, i].rearrange("p h m -> p (h m)"),
                                   start=(c + i == 0), stop=(c == 1 and i == NT - 1))
            mm.then_inc(S("table_sum"), 1)

            def turn_xe(t):
                pe.wait_ge(S("rows_in"), 16 * t + 16)
                for c in range(KD):
                    mm = turn(bank(2 + c // 4)[:, (c % 4) * P:(c % 4 + 1) * P], xg[:, c:D:KD], P)
                mm.then_inc(S("xe_turned"), 1)

            def turn_hid(h):
                for c in (2 * h, 2 * h + 1):
                    mm = turn(bank(4)[:, c * P:(c + 1) * P], hid[:, c * P:(c + 1) * P], P)
                mm.then_inc(S("hid_turned"), 1)

            pe.wait_ge(S("rows_in"), 16)
            for c in range(KD):
                mm = turn(bank(2 + c // 4)[:, (c % 4) * P:(c % 4 + 1) * P], xg[:, c:D:KD], P)
                if c == KD // 2 - 1:
                    mm.then_inc(S("half_turned"), 1)
            mm.then_inc(S("xe_turned"), 1)

            def tile(t, e, last):
                pe.wait_ge(S("xe_lo"), t + 1)
                for h in range(2):
                    for c in range(KD):
                        if h == 0 and c % 2 == 0:
                            wait_lo(pe, e, c // 2)
                        for xs_, ws in ((0, 0), (0, 1), (1, 0)):
                            w = wo[:, ws, c, :].rearrange("p (s f) -> p s f", s=2)[:, :, h * 256:(h + 1) * 256]
                            mm = pe.matmul(bank(h), xe[:, xs_, c, :], w, start=(c == 0 and xs_ + ws == 0),
                                           stop=(c == KD - 1 and xs_ == 1))
                        if h == 0 and c == KD - 1:
                            mm.then_inc(S("first_half"), 1)
                        if h == 1 and c % 2 == 1:
                            mm.then_inc(S("unit_used"), 1)
                        if h == 1 and c == 3:
                            pe.wait_ge(S("hidden"), 2 * t + 1)
                            turn_hid(0)
                turn_xe(t + 1)
                pe.wait_ge(S("he_lo"), 2 * t + 1)
                pe.wait_ge(S("y_copied"), t + 1)
                wait_lo(pe, e, 4)
                for c in range(KF):
                    for hs, ws in ((0, 0), (0, 1), (1, 0)):
                        for h in range(2):
                            mm = pe.matmul(bank(5 + h), he[:, hs, c, :], wd[:, ws, c, h * 512:(h + 1) * 512],
                                           start=(c == 0 and hs + ws == 0), stop=(c == KF - 1 and hs == 1))
                    if c % 2 == 1:
                        mm.then_inc(S("unit_used"), 1)
                    if c == 0:
                        pe.wait_ge(S("hidden"), 2 * t + 2)
                        turn_hid(1)
                    if c == 1:
                        pe.wait_ge(S("he_lo"), 2 * t + 2)
                        wait_lo(pe, e, 5)
            expert_tiles(pe, tile)

            pe.wait_ge(S("tiles_left"), 1)
            for i in range(DVE_WEIGHS, NT):
                M = rows_of(i)
                pe.wait_ge(S("diag_made"), 2 * (i - DVE_WEIGHS + 1))
                pe.wait_ge(S(f"y_back{i % 4}"), 32 * (i // 4 + 1))
                if i >= DVE_WEIGHS + 2:
                    pe.wait_ge(S("out_weighed"), i - 1)
                for c in range(2):
                    for h in range(2):
                        mm = pe.matmul(bank(2 * (i % 2) + h, rows=M), diag[0:M, i % 2, c, 0:M],
                                       yg[2 * (i % 4) + c][0:M, h * 512:(h + 1) * 512], start=(c == 0), stop=(c == 1))
                mm.then_inc(S("y_summed"), 1)


_INS = ["x_prompt", "x_sample", "state_conv_a", "state_pool_b", "state_conv_c", "w_in", "b_in", "conv_a_w",
        "conv_a_b", "ln_a_g", "ln_a_b", "w_pool", "pool_scale", "conv_c_w", "w_out", "b_out", "ln1_g", "ln1_b",
        "w_router_group", "b_router_group", "w_router_expert", "b_router_expert", "w_gate", "w_up", "w_down",
        "ln2_g", "ln2_b"]
_OUTS = [(1, SEQ, D), (DECB, DECT, D), (1, 1, HA, WA), (1, DECB, HA, WA), (1, 1, HB, WB), (1, DECB, HB, WB),
         (1, 1, HC, WC), (1, DECB, HC, WC)]


def kernel(**inputs):
    import numpy as _np
    import concourse.bacc as _bacc
    from concourse import mybir as _mybir
    from concourse.bass_utils import run_bass_kernel_spmd as _run

    nc = _bacc.Bacc("TRN2", target_bir_lowering=False, num_devices=1)
    arrays, args = {}, []
    for name in _INS:
        a = _np.ascontiguousarray(inputs[name])
        arrays[f"in_{name}"] = a
        args.append(nc.dram_tensor(f"in_{name}", a.shape, _mybir.dt.from_np(a.dtype), kind="ExternalInput").ap())
    for i, shape in enumerate(_OUTS):
        args.append(nc.dram_tensor(f"out_{i}", shape, _mybir.dt.float32, kind="ExternalOutput").ap())
    build(nc, *args)
    r = _run(nc, [arrays], core_ids=[0])
    return tuple(r.results[0][f"out_{i}"] for i in range(len(_OUTS)))
```
